# Optimizing a Trainium2 kernel written in Bass

```python
import math
import jax, jax.numpy as jnp
from jax import lax
import numpy as np

D_MODEL = 1024
BATCH = 1
SEQ = 1024
DEPTH = 2

N_MIXERS = 2
N_A_LAYERS = (DEPTH + 1) // 2
N_B_LAYERS = DEPTH // 2

A_HEADS = 16
A_HEAD_DIM = 64
A_WIDTH = A_HEADS * A_HEAD_DIM
DILATION_PAIRS = ((128, 1), (512, 4), (2048, 16))
N_DIL = len(DILATION_PAIRS)
A_QBLOCK = 128
A_IN_COLS = N_DIL * 3 * A_WIDTH + A_WIDTH

SSM_INNER = 2 * D_MODEL
SSM_HEAD_DIM = 64
SSM_HEADS = SSM_INNER // SSM_HEAD_DIM
SSM_STATE = 128
SSM_GROUPS = 4
SSM_CONV = 5
SSM_CHUNK = 128
SSM_CONV_DIM = SSM_INNER + 2 * SSM_GROUPS * SSM_STATE
SSM_IN_COLS = SSM_INNER + SSM_CONV_DIM + 2 * SSM_HEADS

DEEPNORM_ALPHA = (2 * DEPTH) ** 0.25
DEEPNORM_BETA = (8 * DEPTH) ** -0.25
LN_EPS = 1e-5
RMS_EPS = 1e-5

kernel_name = "hybrid_dilated_attn_ssd_encoder"

def _layer_norm(x, g, b):
    xf = x.astype(jnp.float32)
    mu = jnp.mean(xf, axis=-1, keepdims=True)
    var = jnp.mean(jnp.square(xf - mu), axis=-1, keepdims=True)
    y = (xf - mu) * lax.rsqrt(var + LN_EPS) * g.astype(jnp.float32) + b.astype(jnp.float32)
    return y.astype(x.dtype)

def _rms_norm(x, g):
    xf = x.astype(jnp.float32)
    y = xf * lax.rsqrt(jnp.mean(jnp.square(xf), axis=-1, keepdims=True) + RMS_EPS)
    return (y * g.astype(jnp.float32)).astype(x.dtype)

def _alibi_slopes(n):
    return jnp.asarray(2.0 ** (-8.0 * (np.arange(n, dtype=np.float32) + 1.0) / n), dtype=jnp.float32)

def _dilated_group(q, k, v, window, dil, slopes):
    bsz, s, h, dh = q.shape
    length = s // dil
    radius = window // (2 * dil)
    qb = math.gcd(length, A_QBLOCK)
    nblk = length // qb
    span = qb + 2 * radius

    def to_sub(t):
        return t.reshape(bsz, length, dil, h, dh).transpose(0, 2, 3, 1, 4)

    qs = to_sub(q).reshape(bsz, dil, h, nblk, qb, dh)
    pad = ((0, 0), (0, 0), (0, 0), (radius, radius), (0, 0))
    kp = jnp.pad(to_sub(k), pad)
    vp = jnp.pad(to_sub(v), pad)
    idx = np.arange(nblk)[:, None] * qb + np.arange(span)[None, :]
    kb = kp[:, :, :, idx]
    vb = vp[:, :, :, idx]

    scores = jnp.einsum('bdhnqe,bdhnke->bdhnqk', qs, kb).astype(jnp.float32) / math.sqrt(dh)
    delta = np.arange(span)[None, :] - radius - np.arange(qb)[:, None]
    keypos = np.arange(nblk)[:, None, None] * qb + np.arange(span)[None, None, :] - radius
    valid = (np.abs(delta)[None] <= radius) & (keypos >= 0) & (keypos < length)
    dist = jnp.asarray(np.abs(delta) * dil, dtype=jnp.float32)
    alibi = -slopes[:, None, None] * dist[None]
    scores = jnp.where(valid, scores + alibi[None, None, :, None], -jnp.inf)

    m = jnp.max(scores, axis=-1, keepdims=True)
    p = jnp.exp(scores - m)
    z = jnp.sum(p, axis=-1, keepdims=True)
    o = jnp.einsum('bdhnqk,bdhnke->bdhnqe', p.astype(v.dtype), vb) / z.astype(v.dtype)
    lse = (m + jnp.log(z))[..., 0]

    o = o.reshape(bsz, dil, h, length, dh).transpose(0, 3, 1, 2, 4).reshape(bsz, s, h, dh)
    lse = lse.reshape(bsz, dil, h, length).transpose(0, 3, 1, 2).reshape(bsz, s, h)
    return o, lse

def _dilated_attention_mixer(h, w_in, w_out):
    bsz, s, _ = h.shape
    proj = h @ w_in
    qkv = proj[..., :N_DIL * 3 * A_WIDTH].reshape(bsz, s, N_DIL, 3, A_HEADS, A_HEAD_DIM)
    gate = proj[..., N_DIL * 3 * A_WIDTH:]
    slopes = _alibi_slopes(A_HEADS)
    outs, lses = [], []
    for g, (window, dil) in enumerate(DILATION_PAIRS):
        o, l = _dilated_group(qkv[:, :, g, 0], qkv[:, :, g, 1], qkv[:, :, g, 2], window, dil, slopes)
        outs.append(o)
        lses.append(l)
    wts = jax.nn.softmax(jnp.stack(lses, axis=-1), axis=-1).astype(h.dtype)
    o = jnp.einsum('bshg,bshgd->bshd', wts, jnp.stack(outs, axis=3))
    y = o.reshape(bsz, s, A_WIDTH) * jax.nn.silu(gate)
    return y @ w_out

def _segsum_exp(a_cum):
    t = a_cum.shape[-1]
    mask = np.tril(np.ones((t, t), dtype=bool))
    diff = a_cum[..., :, None] - a_cum[..., None, :]
    return jnp.where(mask, jnp.exp(jnp.where(mask, diff, 0.0)), 0.0)

def _ssd_scan(x, dt, a, bm, cm):
    bsz, s, h, p = x.shape
    g, n = bm.shape[-2:]
    rep = h // g
    nc = s // SSM_CHUNK
    xf = x.astype(jnp.float32)
    xg = (xf * dt[..., None]).reshape(bsz, nc, SSM_CHUNK, g, rep, p)
    bc = bm.astype(jnp.float32).reshape(bsz, nc, SSM_CHUNK, g, n)
    cc = cm.astype(jnp.float32).reshape(bsz, nc, SSM_CHUNK, g, n)
    ac = (dt * a).reshape(bsz, nc, SSM_CHUNK, h).transpose(0, 3, 1, 2)
    a_cum = jnp.cumsum(ac, axis=-1)

    lmat = _segsum_exp(a_cum).reshape(bsz, g, rep, nc, SSM_CHUNK, SSM_CHUNK)
    cb = jnp.einsum('bclgn,bcsgn->bgcls', cc, bc)
    y_diag = jnp.einsum('bgrcls,bcsgrp->bclgrp', cb[:, :, None] * lmat, xg)

    decay_states = jnp.exp(a_cum[..., -1:] - a_cum).reshape(bsz, g, rep, nc, SSM_CHUNK)
    states = jnp.einsum('bcsgn,bgrcs,bcsgrp->bcgrpn', bc, decay_states, xg)

    chunk_decay = jnp.moveaxis(jnp.exp(a_cum[..., -1]).reshape(bsz, g, rep, nc), 3, 0)

    def step(hstate, inp):
        dec, st = inp
        return hstate * dec[..., None, None] + st, hstate

    h0 = jnp.zeros((bsz, g, rep, p, n), jnp.float32)
    _, h_prev = lax.scan(step, h0, (chunk_decay, jnp.moveaxis(states, 1, 0)))
    h_prev = jnp.moveaxis(h_prev, 0, 1)

    out_decay = jnp.exp(a_cum).reshape(bsz, g, rep, nc, SSM_CHUNK)
    y_off = jnp.einsum('bclgn,bcgrpn,bgrcl->bclgrp', cc, h_prev, out_decay)
    return (y_diag + y_off).reshape(bsz, s, h, p)

def _ssd_mixer(h, w_in, conv_w, conv_b, dt_bias, a_log, d_skip, norm_w, w_out):
    bsz, s, _ = h.shape
    proj = h @ w_in
    z = proj[..., :SSM_INNER]
    xbc = proj[..., SSM_INNER:SSM_INNER + SSM_CONV_DIM]
    dt_raw = proj[..., SSM_INNER + SSM_CONV_DIM:].astype(jnp.float32)

    half = SSM_CONV // 2
    xbc = lax.conv_general_dilated(
        xbc, conv_w[:, None, :].astype(xbc.dtype), window_strides=(1,), padding=[(half, half)],
        dimension_numbers=('NWC', 'WIO', 'NWC'), feature_group_count=SSM_CONV_DIM)
    xbc = jax.nn.silu(xbc + conv_b)
    xs = xbc[..., :SSM_INNER].reshape(bsz, s, SSM_HEADS, SSM_HEAD_DIM)
    bm = xbc[..., SSM_INNER:SSM_INNER + SSM_GROUPS * SSM_STATE].reshape(bsz, s, SSM_GROUPS, SSM_STATE)
    cm = xbc[..., SSM_INNER + SSM_GROUPS * SSM_STATE:].reshape(bsz, s, SSM_GROUPS, SSM_STATE)

    dtb = dt_bias.astype(jnp.float32)
    dt_f = jax.nn.softplus(dt_raw[..., :SSM_HEADS] + dtb[0])
    dt_b = jax.nn.softplus(dt_raw[..., SSM_HEADS:] + dtb[1])
    a = -jnp.exp(a_log.astype(jnp.float32))

    y_f = _ssd_scan(xs, dt_f, a[0], bm, cm)
    flip = lambda t: jnp.flip(t, axis=1)
    y_b = flip(_ssd_scan(flip(xs), flip(dt_b), a[1], flip(bm), flip(cm)))
    y = y_f + y_b + d_skip.astype(jnp.float32)[:, None] * xs.astype(jnp.float32)
    y = y.astype(h.dtype).reshape(bsz, s, SSM_INNER) * jax.nn.silu(z)
    y = _rms_norm(y, norm_w)
    return y @ w_out

def setup_inputs(seed: int = 0) -> dict:
    key = jax.random.key(seed)
    ks = jax.random.split(key, 20)
    f32 = jnp.float32
    nrm = lambda k, shape, scale: jax.random.normal(k, shape, f32) * scale

    x = jax.random.normal(ks[0], (BATCH, SEQ, D_MODEL), f32)
    c = jax.random.normal(ks[1], (BATCH, D_MODEL), f32)
    ada_w = nrm(ks[2], (DEPTH, D_MODEL, 3 * D_MODEL), D_MODEL ** -0.5)
    ada_b = nrm(ks[3], (DEPTH, 3 * D_MODEL), 0.02)
    ln_g = 1.0 + nrm(ks[4], (DEPTH, D_MODEL), 0.02)
    ln_b = nrm(ks[5], (DEPTH, D_MODEL), 0.02)

    a_w_in = nrm(ks[6], (N_A_LAYERS, D_MODEL, A_IN_COLS), D_MODEL ** -0.5)
    a_w_out = nrm(ks[7], (N_A_LAYERS, A_WIDTH, D_MODEL), DEEPNORM_BETA * A_WIDTH ** -0.5)

    b_w_in = nrm(ks[8], (N_B_LAYERS, D_MODEL, SSM_IN_COLS), D_MODEL ** -0.5)
    b_conv_w = nrm(ks[9], (N_B_LAYERS, SSM_CONV, SSM_CONV_DIM), SSM_CONV ** -0.5)
    b_conv_b = nrm(ks[10], (N_B_LAYERS, SSM_CONV_DIM), 0.02)
    dt0 = jnp.exp(jax.random.uniform(ks[11], (N_B_LAYERS, 2, SSM_HEADS), f32,
                                     math.log(1e-3), math.log(1e-1)))
    b_dt_bias = dt0 + jnp.log(-jnp.expm1(-dt0))
    b_a_log = jnp.log(jax.random.uniform(ks[12], (N_B_LAYERS, 2, SSM_HEADS), f32, 1.0, 16.0))
    b_d = 1.0 + nrm(ks[13], (N_B_LAYERS, SSM_HEADS), 0.02)
    b_norm_w = 1.0 + nrm(ks[14], (N_B_LAYERS, SSM_INNER), 0.02)
    b_w_out = nrm(ks[15], (N_B_LAYERS, SSM_INNER, D_MODEL), DEEPNORM_BETA * SSM_INNER ** -0.5)

    return {"x": x, "c": c, "ada_w": ada_w, "ada_b": ada_b, "ln_g": ln_g, "ln_b": ln_b,
            "a_w_in": a_w_in, "a_w_out": a_w_out,
            "b_w_in": b_w_in, "b_conv_w": b_conv_w, "b_conv_b": b_conv_b,
            "b_dt_bias": b_dt_bias, "b_a_log": b_a_log, "b_d": b_d,
            "b_norm_w": b_norm_w, "b_w_out": b_w_out}

def reference(x, c, ada_w, ada_b, ln_g, ln_b, a_w_in, a_w_out,
              b_w_in, b_conv_w, b_conv_b, b_dt_bias, b_a_log, b_d, b_norm_w, b_w_out):
    cond = jax.nn.silu(c)
    for i in range(DEPTH):
        mod = cond @ ada_w[i] + ada_b[i]
        shift, scale, gate = jnp.split(mod, 3, axis=-1)
        h = x * (1.0 + scale[:, None, :]) + shift[:, None, :]
        j = i // N_MIXERS
        if i % N_MIXERS == 0:
            y = _dilated_attention_mixer(h, a_w_in[j], a_w_out[j])
        else:
            y = _ssd_mixer(h, b_w_in[j], b_conv_w[j], b_conv_b[j], b_dt_bias[j],
                           b_a_log[j], b_d[j], b_norm_w[j], b_w_out[j])
        x = _layer_norm(DEEPNORM_ALPHA * x + gate[:, None, :] * y, ln_g[i], ln_b[i])
    return x


_drawn_inputs = setup_inputs


def setup_inputs(seed=0):
    import zlib

    import numpy as np

    out = dict(_drawn_inputs(seed))
    spreads = {}
    factors = {'ada_b': 4.64, 'b_conv_b': 8.0, 'b_d': 8.0, 'b_norm_w': 8.0}
    for name, (base, spread) in spreads.items():
        noise = np.random.default_rng([zlib.crc32(name.encode()), seed]).standard_normal(out[name].shape)
        drawn = base * np.exp(spread * noise) if base else spread * noise
        out[name] = __import__('jax').numpy.asarray(drawn.astype(out[name].dtype))
    for name, factor in factors.items():
        out[name] = (out[name] * factor).astype(out[name].dtype)
    return out
```

```python
import math
from contextlib import ExitStack

import concourse.bass as bass
from concourse import mybir

F32 = mybir.dt.float32
F32R = mybir.dt.float32r
ALU = mybir.AluOpType
ACT = mybir.ActivationFunctionType
AX = mybir.AxisListType.X

P = 128
SEQ = 1024
D = 1024
KT = D // P
HALF = 512
DEPTH = 2
ALPHA = (2 * DEPTH) ** 0.25
LN_EPS = 1e-5
RMS_EPS = 1e-5

HEADS, HD = 16, 64
PAIRS = HEADS // 2
DILS = (1, 4, 16)
RADIUS = 64
MASKED = -2.0 ** 100
KC0 = SEQ + 2 * RADIUS
VT2, Q2, K2, VT0, Q0, K0, GATE, VT1, Q1, K1 = range(10)
FIRST_TILES = (VT0, Q0, K0, VT1, Q1, K1)
LAST_TILES = (VT2, Q2, K2, GATE)
TILE_GROUP = {VT2: (2, 2), Q2: (2, 0), K2: (2, 1), VT0: (0, 2), Q0: (0, 0), K0: (0, 1),
              VT1: (1, 2), Q1: (1, 0), K1: (1, 1)}
UNITS = 20
TILES_A = 10 * PAIRS


def stream_a():
    def col(kind, pair):
        if kind == GATE:
            return 9 * D + pair * P
        g, which = TILE_GROUP[kind]
        return (3 * g + which) * D + pair * P
    order = [col(k, 0) for k in FIRST_TILES]
    for j in range(PAIRS):
        if j < PAIRS - 1:
            order += [col(k, j + (k in FIRST_TILES)) for k in range(10)]
        else:
            order += [col(k, j) for k in LAST_TILES]
    return order


def unit_of(u):
    if u < 16:
        return u // 8, u % 2, 2 * (u % 8 // 2), 2, 256
    return 2, u % 2, 4 * ((u - 16) // 2), 4, 128


def bias_tables():
    import numpy as np
    q = np.arange(P)[:, None]
    c = np.arange(256)[None, :]
    out = []
    for first, last in ((True, False), (False, False), (False, True)):
        d = np.abs(c - RADIUS - q)
        ok = (d <= RADIUS) & (c >= RADIUS * first) & (c < 256 - RADIUS * last)
        out.append(np.where(ok, -d, MASKED))
    wide = np.arange(384)[None, :]
    d = np.abs(wide - P - q)
    out.append(np.where(d <= RADIUS, -4.0 * d, MASKED))
    c = np.arange(P)[None, :]
    out.append(np.where(q // 64 == c // 64, -16.0 * np.abs(q % 64 - c % 64), MASKED))
    return np.concatenate(out, 1).astype(np.float32)


def bias_columns(g, n):
    if g == 0:
        return 256 * (0 if n == 0 else 2 if n == 7 else 1), 256
    if g == 1:
        return 768 + P * (1 - n % 2), 256
    return 1152, P


class Chain:

    def __init__(self, eng, sem, base):
        self.eng, self.sem, self.base, self.n = eng, sem, base, 0

    def link(self, ins):
        self.n += 1
        ins.then_inc(self.sem, 1)
        self.eng.wait_ge(self.sem, self.base + self.n)


def bcast(ap, n):
    return ap.unsqueeze(len(ap.shape)).broadcast_to(list(ap.shape) + [n])


def modulation_phase(nc, io, keep):
    with ExitStack() as ctx:
        def sb(name, shape, dt=F32):
            return ctx.enter_context(nc.sbuf_tensor(name, shape, dt))

        def sem(name):
            return ctx.enter_context(nc.semaphore(name))

        RING = 3
        w_ring = sb("ada_ring", [P, RING, 3 * D])
        acc = sb("ada_acc", [P, 2, 3 * D])
        cc = sb("c_cols", [P, 4, KT])
        brow = sb("ada_b_rows", [1, DEPTH, 3 * D])
        ones = sb("ones", [P, P])
        gate_sb = sb("gate_sb", [P, DEPTH, D])
        x_ring = sb("xT_ring", [P, 2, SEQ])
        h_tmp = sb("h_tmp", [P, 2, SEQ])
        ps_col = ctx.enter_context(nc.psum_tensor("ps_col", [P, DEPTH, HALF], F32))
        ps_gate = ctx.enter_context(nc.psum_tensor("ps_gate", [P, DEPTH * 2, HALF], F32))

        c_in, b_in, c_exp = sem("c_in"), sem("b_in"), sem("c_exp")
        ones_set = sem("ones_set")
        w_in = [sem(f"ada_in{i}") for i in range(RING)]
        w_used = sem("ada_used")
        acc_done, col_full, mods_ready = sem("acc_done"), sem("col_full"), sem("mods_ready")
        gate_full, gate_copied, gate_out = sem("gate_full"), sem("gate_copied"), sem("gate_out")
        x_in = [sem("xT_in0"), sem("xT_in1")]
        h_made, h_hi, h_lo, v_step = sem("h_made"), sem("h_hi"), sem("h_lo"), sem("v_step0")

        block = ctx.enter_context(nc.Block())

        @block.sync
        def _(sp):
            sp.dma_start(cc[:, 0, :], io["c"]).then_inc(c_in, 16)
            for i in range(DEPTH * KT):
                if i >= RING:
                    sp.wait_ge(w_used, i - RING + 1)
                sp.dma_start(w_ring[:, i % RING, :],
                             io["ada_w"][i // KT, P * (i % KT):P * (i % KT) + P, :]
                             ).then_inc(w_in[i % RING], 16)
                if i == 0:
                    sp.dma_start(brow[:], io["ada_b"]).then_inc(b_in, 16)

        @block.gpsimd
        def _(pool):
            pool.memset(ones[:], 1.0).then_inc(ones_set, 1)
            for k in range(KT):
                pool.wait_ge(h_hi, k + 1)
                nc.gpsimd.tensor_tensor(keep["h_lo"][:, k, :], h_tmp[:, k % 2, :],
                                        keep["h_hi"][:, k, :].bitcast(F32),
                                        ALU.subtract).then_inc(h_lo, 1)

        @block.scalar
        def _(act):
            for k in range(2):
                act.dma_start(x_ring[:, k, :], io["xT"][:, k, :]).then_inc(x_in[k], 16)
            act.wait_ge(c_in, 16)
            nc.scalar.activation(cc[:, 1, :], cc[:, 0, :], ACT.Exp, scale=-1.0).then_inc(c_exp, 1)
            for k in range(KT):
                act.wait_ge(h_made, k + 1)
                nc.scalar.activation(keep["h_hi"][:, k, :], h_tmp[:, k % 2, :],
                                     ACT.Copy).then_inc(h_hi, 1)
                if k + 2 < KT:
                    act.dma_start(x_ring[:, k % 2, :], io["xT"][:, k + 2, :]).then_inc(x_in[k % 2], 16)
            for layer in range(DEPTH):
                act.wait_ge(gate_copied, layer + 1)
                act.dma_start(io["gate_rows"][layer:layer + 1, :],
                              gate_sb[0:1, layer, :]).then_inc(gate_out, 16)
            act.wait_ge(gate_out, 16 * DEPTH)

        @block.vector
        def _(dve):
            ch = Chain(dve, v_step, 0)
            dve.wait_ge(c_exp, 1)
            ch.link(nc.vector.tensor_scalar(cc[:, 2, :], cc[:, 1, :], 1.0, None, ALU.add))
            ch.link(nc.vector.reciprocal(cc[:, 3, :], cc[:, 2, :]))
            ch.link(nc.vector.tensor_tensor(cc[:, 1, :], cc[:, 0, :], cc[:, 3, :], ALU.mult))
            for i in range(DEPTH * KT):
                layer, k = i // KT, i % KT
                dve.wait_ge(w_in[i % RING], 16 * (i // RING + 1))
                if k == 0:
                    ins = nc.vector.tensor_scalar(acc[:, layer, :], w_ring[:, i % RING, :],
                                                  cc[:, 1, k:k + 1], None, ALU.mult)
                else:
                    dve.wait_ge(w_used, i)
                    ins = nc.vector.scalar_tensor_tensor(
                        acc[:, layer, :], w_ring[:, i % RING, :], cc[:, 1, k:k + 1],
                        acc[:, layer, :], ALU.mult, ALU.add)
                ins.then_inc(w_used, 1)
                if k == KT - 1:
                    dve.wait_ge(col_full, layer + 1)
                    ins = nc.vector.tensor_copy(keep["mods"][:, layer, :], ps_col[:, layer, 0:2 * KT])
                    ch.link(ins)
                    nc.vector.tensor_scalar(keep["mods"][:, layer, KT:2 * KT],
                                            keep["mods"][:, layer, KT:2 * KT], 1.0, None,
                                            ALU.add).then_inc(mods_ready, 1)
                    dve.wait_ge(gate_full, layer + 1)
                    nc.vector.tensor_copy(gate_sb[:, layer, :].rearrange("p (a b) -> p a b", a=2),
                                          ps_gate[:, 2 * layer:2 * layer + 2, :]).then_inc(gate_copied, 1)
                if i == KT - 1:
                    dve.wait_ge(mods_ready, 1)
                    for kk in range(KT):
                        dve.wait_ge(x_in[kk % 2], 16 * (kk // 2 + 1))
                        if kk >= 2:
                            dve.wait_ge(h_lo, kk - 1)
                        nc.vector.tensor_scalar(h_tmp[:, kk % 2, :], x_ring[:, kk % 2, :],
                                                keep["mods"][:, 0, KT + kk:KT + kk + 1],
                                                keep["mods"][:, 0, kk:kk + 1],
                                                ALU.mult, ALU.add).then_inc(h_made, 1)

        @block.tensor
        def _(pe):
            pe.wait_ge(ones_set, 1)
            pe.wait_ge(b_in, 16)
            for layer in range(DEPTH):
                pe.wait_ge(w_used, KT * (layer + 1))
                for n in range(2 * KT):
                    nc.tensor.matmul(ps_col[:, layer, n:n + 1], acc[:, layer, n * P:(n + 1) * P],
                                     ones[:, 0:1], start=True, stop=False)
                    last = nc.tensor.matmul(ps_col[:, layer, n:n + 1],
                                            brow[0:1, layer, n * P:(n + 1) * P],
                                            ones[0:1, 0:1], start=False, stop=True)
                last.then_inc(col_full, 1)
                for n in range(2):
                    c0 = 2 * D + n * HALF
                    nc.tensor.matmul(ps_gate[:, 2 * layer + n, :], ones[:],
                                     acc[:, layer, c0:c0 + HALF], start=True, stop=False)
                    last = nc.tensor.matmul(ps_gate[:, 2 * layer + n, :], ones[0:1, :],
                                            brow[0:1, layer, c0:c0 + HALF], start=False, stop=True)
                last.then_inc(gate_full, 1)


def attention_phase(nc, io, keep):
    with ExitStack() as ctx:
        def sb(name, shape, dt=F32):
            return ctx.enter_context(nc.sbuf_tensor(name, shape, dt))

        def ps(name, shape):
            return ctx.enter_context(nc.psum_tensor(name, shape, F32))

        def sem(name):
            return nc.alloc_semaphore(name)

        w_raw = sb("w_raw", [P, 2, KT, P])
        w_hi = sb("w_hi", [P, 2, KT, P], F32R)
        w_lo = sb("w_lo", [P, 2, KT, P], F32R)
        qT = [sb(f"qT{g}", [P, SEQ]) for g in range(3)]
        kT = [sb(f"kT{g}", [P, KC0 if g == 0 else SEQ]) for g in range(3)]
        vT = sb("vT", [P, SEQ])
        v = [sb(f"v{g}", [P, 8, P]) for g in range(3)]
        gate = sb("gate", [P, SEQ])
        bias = sb("bias", [P, 1280])
        ident = sb("ident", [P, P])
        slope = sb("slope", [P, 2])
        qscale = sb("qscale", [P, 2])
        prob = sb("prob", [P, 2, HALF])
        probT = sb("probT", [P, 2, HALF])
        top = sb("top", [P, 4, 4])
        ntop = sb("ntop", [P, 4, 4])
        z = sb("z", [P, 4, 4])
        rz = sb("rz", [P, 4, 4])
        lnz = sb("lnz", [P, 4, 4])
        o_st = sb("o_st", [P, 4, P])
        lse = sb("lse", [P, 4, P])
        stage = sb("stage", [P, 2, 2, 256])
        num = sb("num", [P, SEQ])
        den = sb("den", [P, SEQ])
        ref = sb("ref", [P, SEQ])
        ee = sb("ee", [P, 2, 2, 256])
        mx = sb("mx", [P, 2, 256])

        pp = ps("pp", [P, 2, HALF])
        sp_ = ps("sp_", [P, 2, HALF])
        tp = ps("tp", [P, 2, HALF])
        op = ps("op", [P, 2, 256])
        ot = ps("ot", [P, HALF])

        const_in = sem("const_in")
        w_in = [sem("w_in0"), sem("w_in1")]
        hi_done, lo_done = sem("hi_done"), sem("lo_done")
        pp_full, pp_free = sem("pp_full"), sem("pp_free")
        s_full, s_free = sem("s_full"), sem("s_free")
        tops_begun = sem("tops_begun")
        top_ready, p_ready, lnz_ready = sem("top_ready"), sem("p_ready"), sem("lnz_ready")
        t_full, t_free = sem("t_full"), sem("t_free")
        o_full, o_free, o_ready = sem("o_full"), sem("o_free"), sem("o_ready")
        ot_full, ot_free = sem("ot_full"), sem("ot_free")
        diff_ready, wt_ready, stage_used = sem("diff_ready"), sem("wt_ready"), sem("stage_used")
        den_ready, den_inverse, y_done = sem("den_ready"), sem("den_inverse"), sem("y_done")
        g_step, y_begun = sem("g_step"), sem("y_begun")
        scale_set = sem("scale_set")
        v_step = sem("v_step1")

        V_AT = {3: 2, 9: 0, 17: 1}

        def t_events(steps=UNITS, v_at=V_AT):
            out = []
            for u in range(steps):
                out.append(("p", u))
                if u in v_at:
                    out += [("v", v_at[u], 0), ("v", v_at[u], 1)]
            return out

        T_EVENTS = t_events()
        NT = len(T_EVENTS)
        T_AT = {e: n for n, e in enumerate(T_EVENTS)}
        T_LAST = {e: n for n, e in enumerate(t_events(v_at={3: 2}))}
        T0 = 4
        OT_BY_UNIT = {u: ([u // 2] if u < 16 else [8 + (u - 17), 9 + (u - 17)])
                      for u in range(1, UNITS, 2)}
        NE = 12
        TILE_OF_UNIT = lambda u: u // 2
        STEP_TILES = tuple(range(10))

        def tokens(buf, e):
            if e < 4:
                return buf[:, 256 * e:256 * e + 256]
            if e < 8:
                return buf[:, :].rearrange("p (i r) -> p r i", r=4)[:, e - 4, :]
            m = e - 8
            return buf[:, :].rearrange("p (i r) -> p r i", r=16)[:, 4 * m:4 * m + 4, :]

        def like(flat, e):
            return flat if e < 8 else flat.rearrange("p (r i) -> p r i", r=4)

        block = ctx.enter_context(nc.Block())

        @block.sync
        def _(sp):
            def load(n, slot):
                sp.dma_start(w_raw[:, slot], io["a_w"][n]).then_inc(w_in[slot], 16)

            load(0, 0)
            load(1, 1)
            sp.dma_start(bias[:], io["bias"]).then_inc(const_in, 16)
            sp.dma_start(ident[:], io["ident"]).then_inc(const_in, 16)
            sp.dma_start(slope[:], io["slope"]).then_inc(const_in, 16)
            sp.dma_start(qscale[:], io["qscale"]).then_inc(const_in, 16)
            for n in range(2, 6):
                sp.wait_ge(lo_done, n - 1)
                load(n, n % 2)
            with sp.Fori(0, PAIRS - 1) as j:
                for f in range(10):
                    sp.wait_ge(lo_done, 10 * j + (6 + f - 1))
                    load(10 * j + (6 + f), f % 2)
            for f in range(4):
                n = 10 * (PAIRS - 1) + 6 + f
                sp.wait_ge(lo_done, n - 1)
                load(n, f % 2)

        @block.gpsimd
        def _(pool):
            def split_lo(n, slot):
                pool.wait_ge(hi_done, n + 1)
                nc.gpsimd.tensor_tensor(w_lo[:, slot].rearrange("p k c -> p (k c)"),
                                        w_raw[:, slot].rearrange("p k c -> p (k c)"),
                                        w_hi[:, slot].rearrange("p k c -> p (k c)").bitcast(F32),
                                        ALU.subtract).then_inc(lo_done, 1)
            def merge(ch, j, e):
                if e == 8:
                    pool.wait_ge(stage_used, 4 * j + 4)
                pool.wait_ge(wt_ready, 8 * j + (e - 3))
                e0, e1 = (like(ee[:, e % 2, i, :], e) for i in range(2))
                st, g = like(stage[:, e % 2, 0, :], e), like(mx[:, e % 2, :], e)
                nv, dv = tokens(num, e), tokens(den, e)
                nc.gpsimd.tensor_tensor(nv, nv, e0, ALU.mult)
                ch.link(nc.gpsimd.tensor_tensor(st, st, e1, ALU.mult))
                if e < 8:
                    nc.gpsimd.tensor_tensor(dv, e0, e1, ALU.add)
                    nc.gpsimd.tensor_tensor(nv, nv, st, ALU.add).then_inc(stage_used, 1)
                    return
                nc.gpsimd.tensor_tensor(nv, nv, st, ALU.add)
                ch.link(nc.gpsimd.tensor_tensor(dv, dv, e0, ALU.mult))
                nc.gpsimd.tensor_tensor(nv, nv, tokens(gate, e), ALU.mult)
                ch.link(nc.gpsimd.tensor_tensor(dv, dv, e1, ALU.add))
                ch.link(nc.gpsimd.tensor_tensor(g, g, dv, ALU.mult))
                nc.gpsimd.tensor_tensor(dv, dv, g, ALU.add).then_inc(den_ready, 1)

            def gated(j, e):
                pool.wait_ge(den_inverse, 4 * j + (e - 7))
                pool.sem_inc(y_begun, 1)
                y = keep["y"][:, j, :] if isinstance(j, int) else keep["y"][
                    :, bass.ds(j, 1), :].rearrange("p a t -> p (a t)")
                nc.gpsimd.tensor_tensor(tokens(y, e), tokens(num, e), tokens(den, e),
                                        ALU.mult).then_inc(y_done, 1)

            pool.sem_inc(y_done, 1)
            pool.sem_inc(den_ready, 2)
            for n in range(8):
                split_lo(n, n % 2)

            def pair(ch, j, splits):
                for u in range(2, UNITS):
                    f = u // 2 + 1
                    if u % 2 == 0 and f <= splits:
                        split_lo(10 * j + (6 + f), f % 2)
                    if u % 2 == 0 and OT_BY_UNIT[u - 1][0] >= 4:
                        merge(ch, j, OT_BY_UNIT[u - 1][0])
                    if u == UNITS - 2:
                        merge(ch, j, OT_BY_UNIT[u - 1][1])
                gated(j, 8)
                merge(ch, j, 10)
                gated(j, 9)
                merge(ch, j, 11)

            POOL_STEPS = 4 + 4 * 4
            with pool.Fori(0, PAIRS - 1) as j:
                ch = Chain(pool, g_step, POOL_STEPS * j)
                pair(ch, j, 10)
                assert ch.n == POOL_STEPS, ch.n
                split_lo(10 * j + 17, 1)
                gated(j, 10)
                gated(j, 11)
            pair(Chain(pool, g_step, POOL_STEPS * (PAIRS - 1)), PAIRS - 1, 3)
            gated(PAIRS - 1, 10)
            gated(PAIRS - 1, 11)

        @block.tensor
        def _(pe):
            def project(unit, par, tile, slot, half, part):
                if part == 0:
                    pe.wait_ge(lo_done, tile + 1)
                    pe.wait_ge(pp_free, unit + 1)
                for k in (2 * part, 2 * part + 1):
                    for n, (w, h) in enumerate(((w_hi, "h_hi"), (w_hi, "h_lo"), (w_lo, "h_hi"))):
                        last = nc.tensor.matmul(
                            pp[:, par, :], w[:, slot, k, :],
                            keep[h][:, k, half * HALF:(half + 1) * HALF],
                            start=(k == 0 and n == 0), stop=(k == KT - 1 and n == 2))
                if part == 3:
                    last.then_inc(pp_full, 1)

            def scores(j, u):
                g, h, n0, nt, w = unit_of(u)
                if u == 0:
                    pe.wait_ge(pp_free, 20 * j + 8)
                if u == 8:
                    pe.wait_ge(pp_free, 20 * j + 14)
                if u == 16:
                    pe.wait_ge(pp_free, 20 * j + 20)
                pe.wait_ge(s_free, UNITS * j + (u + 1))
                rows = slice(HD * h, HD * h + HD)
                for t in range(nt):
                    n = n0 + t
                    k0 = (P * n, 256 * (n // 2), P * n)[g]
                    last = nc.tensor.matmul(sp_[:, u % 2, t * w:(t + 1) * w],
                                            qT[g][rows, P * n:P * n + P],
                                            kT[g][rows, k0:k0 + w], start=True, stop=True)
                last.then_inc(s_full, 1)

            def transpose_probs(j, u, at, par):
                pe.wait_ge(p_ready, UNITS * j + (u + 1))
                pe.wait_ge(t_free, T0 + at + 1)
                for c in range(4):
                    last = nc.tensor.transpose(tp[:, par, c * P:(c + 1) * P],
                                               prob[:, u % 2, c * P:(c + 1) * P], ident[:])
                last.then_inc(t_full, 1)

            def transpose_v(at, par, half, units_done):
                pe.wait_ge(pp_free, units_done)
                pe.wait_ge(t_free, at + 1)
                for c in range(4):
                    c0 = half * HALF + c * P
                    last = nc.tensor.transpose(tp[:, par, c * P:(c + 1) * P],
                                               vT[:, c0:c0 + P], ident[:])
                last.then_inc(t_full, 1)

            def values(j, u, at):
                g, h, n0, nt, w = unit_of(u)
                pe.wait_ge(t_free, T0 + at + 3)
                pe.wait_ge(o_free, UNITS * j + (u + 1))
                for t in range(nt):
                    n = n0 + t
                    keys = ((n, (n + 1) % 8), (n // 2 * 2, n // 2 * 2 + 1), (n,))[g]
                    for i, kt in enumerate(keys):
                        c = t * len(keys) + i
                        last = nc.tensor.matmul(op[:, u % 2, t * HD:(t + 1) * HD],
                                                probT[:, u % 2, c * P:(c + 1) * P],
                                                v[g][:, kt, HD * h:HD * h + HD],
                                                start=(i == 0), stop=(i == len(keys) - 1))
                last.then_inc(o_full, 1)

            def merge_transposes(j, u, e):
                t0 = 2 * (e - OT_BY_UNIT[u][0])
                pe.wait_ge(o_ready, UNITS * j + (u + 1))
                pe.wait_ge(ot_free, NE * j + (e + 1))
                for t in range(2):
                    nc.tensor.transpose(ot[:, t * P:(t + 1) * P], o_st[:, t0 + t, :], ident[:])
                    last = nc.tensor.transpose(ot[:, 256 + t * P:256 + (t + 1) * P],
                                               lse[:, t0 + t, :], ident[:])
                last.then_inc(ot_full, 1)

            pe.wait_ge(const_in, 64)
            for un in range(12):
                for part in range(4):
                    project(un, un % 2, un // 2, un // 2 % 2, un % 2, part)
                if un in (3, 9):
                    for half in range(2):
                        at = (0 if un == 3 else 2) + half
                        transpose_v(at, at % 2, half, (4 if un == 3 else 10))
            scores(0, 0)
            scores(0, 1)

            def pair(j, table, tiles, last_pair):
                base_u = 20 * j + 12
                base_t = NT * j

                def proj(u, part):
                    if u < 2 * tiles:
                        project(base_u + u, u % 2, 10 * j + (6 + u // 2), (u // 2) % 2, u % 2, part)

                def probs_t(u):
                    n = table[("p", u)]
                    transpose_probs(j, u, base_t + n, n % 2)

                for u in range(UNITS):
                    if 1 <= u < UNITS - 1:
                        scores(j, u + 1)
                    if u == UNITS - 1:
                        probs_t(u)
                    if u % 2 == 0 and u >= 2:
                        merge_transposes(j, u - 1, OT_BY_UNIT[u - 1][0])
                    proj(u, 0)
                    proj(u, 1)
                    if u < UNITS - 1:
                        probs_t(u)
                    else:
                        values(j, u, base_t + table[("p", u)])
                    if u == UNITS - 2:
                        merge_transposes(j, u - 1, OT_BY_UNIT[u - 1][1])
                    proj(u, 2)
                    if u == UNITS - 1:
                        merge_transposes(j, u, OT_BY_UNIT[u][0])
                    proj(u, 3)
                    if u < UNITS - 1:
                        values(j, u, base_t + table[("p", u)])
                    if u in V_AT and ("v", V_AT[u], 0) in table:
                        for half in range(2):
                            n = table[("v", V_AT[u], half)]
                            transpose_v(base_t + (T0 + n), n % 2, half, base_u + (u + 1))
                if not last_pair:
                    scores(j + 1, 0)
                merge_transposes(j, UNITS - 1, OT_BY_UNIT[UNITS - 1][1])
                if not last_pair:
                    scores(j + 1, 1)

            with pe.Fori(0, PAIRS - 1) as j:
                pair(j, T_AT, 10, False)
            pair(PAIRS - 1, T_LAST, 4, True)

        @block.scalar
        def _(act):
            def split_hi(n, slot, rounds):
                act.wait_ge(w_in[slot], rounds * 16)
                act.wait_ge(pp_full, 2 * (n - 2) + 2)
                nc.scalar.activation(w_hi[:, slot].rearrange("p k c -> p (k c)"),
                                     w_raw[:, slot].rearrange("p k c -> p (k c)"),
                                     ACT.Copy).then_inc(hi_done, 1)

            def put(dst, src, **kw):
                return nc.scalar.activation(dst, src, ACT.Copy, **kw)

            def evacuate(j, unit, par, kind, half, scale_col):
                act.wait_ge(pp_full, unit + 1)
                src = pp[:, par, :]
                t0 = half * HALF
                if kind == GATE:
                    if half == 0:
                        act.wait_ge(y_done, 4 * j + 1)
                    put(gate[:, t0:t0 + HALF], src).then_inc(pp_free, 1)
                    return
                g, which = TILE_GROUP[kind]
                buf = (qT[g], kT[g], vT)[which]
                kw = {"scale": qscale[:, scale_col:scale_col + 1]} if which == 0 else {}
                if g == 0 and which > 0:
                    if half == 0:
                        if which == 1:
                            put(buf[:, SEQ + RADIUS:KC0], src[:, 0:RADIUS])
                        ins = put(buf[:, RADIUS:RADIUS + HALF], src)
                    elif which == 1:
                        put(buf[:, 0:RADIUS], src[:, HALF - RADIUS:HALF])
                        ins = put(buf[:, RADIUS + HALF:RADIUS + SEQ], src)
                    else:
                        put(buf[:, 0:RADIUS], src[:, HALF - RADIUS:HALF])
                        ins = put(buf[:, RADIUS + HALF:SEQ], src[:, 0:HALF - RADIUS])
                elif g == 0:
                    ins = put(buf[:, t0:t0 + HALF], src, **kw)
                else:
                    d = DILS[g]
                    dst = buf[:, 0:SEQ].rearrange("p (r i) -> p i r", r=d)
                    ins = put(dst[:, t0 // d:(t0 + HALF) // d, :],
                              src.rearrange("p (i r) -> p i r", r=d), **kw)
                ins.then_inc(pp_free, 1)

            def softmax(j, u):
                g, h, n0, nt, w = unit_of(u)
                act.wait_ge(top_ready, UNITS * j + (u + 1))
                for t in range(nt):
                    last = nc.scalar.activation(prob[:, u % 2, t * w:(t + 1) * w],
                                                prob[:, u % 2, t * w:(t + 1) * w], ACT.Exp,
                                                bias=ntop[:, u % 4, t:t + 1],
                                                accum_out=z[:, u % 4, t:t + 1])
                last.then_inc(p_ready, 1)
                act.wait_ge(p_ready, UNITS * j + (u + 1))
                nc.scalar.activation(lnz[:, u % 4, 0:nt], z[:, u % 4, 0:nt],
                                     ACT.Ln).then_inc(lnz_ready, 1)

            def weights(j, u, e):
                if e >= 4:
                    act.wait_ge(diff_ready, 8 * j + (e - 3))
                    if e >= 8:
                        nc.scalar.activation(like(mx[:, e % 2, :], e), tokens(gate, e), ACT.Exp,
                                             scale=-1.0)
                    flat = ee[:, e % 2].rearrange("p a c -> p (a c)")
                    nc.scalar.activation(flat, flat, ACT.Exp).then_inc(wt_ready, 1)

            act.preload_act_table_set("natural_log_exp_and_others")
            act.sem_inc(pp_free, 2)
            act.wait_ge(const_in, 64)
            act.wait_ge(w_in[0], 16)
            nc.scalar.activation(w_hi[:, 0].rearrange("p k c -> p (k c)"),
                                 w_raw[:, 0].rearrange("p k c -> p (k c)"),
                                 ACT.Copy).then_inc(hi_done, 1)
            for un in range(12):
                if un >= 1:
                    if un - 1 == 6:
                        act.wait_ge(t_full, 2)
                    evacuate(0, un - 1, (un - 1) % 2, FIRST_TILES[(un - 1) // 2], (un - 1) % 2, 0)
                if un % 2 == 0:
                    n = un // 2 + 1
                    act.wait_ge(w_in[n % 2], 16 * (n // 2 + 1))
                    if n >= 2:
                        act.wait_ge(pp_full, 2 * (n - 2) + 2)
                    nc.scalar.activation(w_hi[:, n % 2].rearrange("p k c -> p (k c)"),
                                         w_raw[:, n % 2].rearrange("p k c -> p (k c)"),
                                         ACT.Copy).then_inc(hi_done, 1)
            evacuate(0, 11, 1, K1, 1, 0)
            softmax(0, 0)

            def pair(j, table, kinds, last_pair):
                base_u = 20 * j + 12
                units = 2 * len(kinds)
                for u in range(UNITS):
                    if 1 <= u <= units:
                        k = kinds[(u - 1) // 2]
                        first_half = (u - 1) % 2 == 0
                        if k in (VT2, VT0, VT1) and first_half:
                            before = {VT2: None, VT0: ("v", 2, 1), VT1: ("v", 0, 1)}[k]
                            act.wait_ge(t_full, T0 + NT * j + (table[before] + 1 if before else 0))
                        evacuate(j, base_u + (u - 1), (u - 1) % 2, k, (u - 1) % 2,
                                 0 if k == Q2 else 1)
                    if u >= 1:
                        softmax(j, u)
                    if u % 2 == 0 and (not last_pair or u // 2 + 1 < len(kinds)):
                        f = u // 2 + 1
                        split_hi(10 * j + (6 + f), f % 2, 5 * j + (3 + f // 2 + 1))
                    if u % 2 == 0 and u >= 2:
                        weights(j, u - 1, OT_BY_UNIT[u - 1][0])
                    if u == UNITS - 2:
                        weights(j, u - 1, OT_BY_UNIT[u - 1][1])
                if not last_pair:
                    evacuate(j, base_u + 19, 1, kinds[9], 1, 1)
                    softmax(j + 1, 0)
                weights(j, UNITS - 1, OT_BY_UNIT[UNITS - 1][0])
                weights(j, UNITS - 1, OT_BY_UNIT[UNITS - 1][1])
                if not last_pair:
                    nc.scalar.activation(qscale[:], qscale[:], ACT.Copy,
                                         scale=2.0).then_inc(scale_set, 1)
                    act.wait_ge(scale_set, j + 1)

            with act.Fori(0, PAIRS - 1) as j:
                pair(j, T_AT, STEP_TILES, False)
            pair(PAIRS - 1, T_LAST, LAST_TILES, True)

        @block.vector
        def _(dve):
            def tops(ch, j, u):
                g, h, n0, nt, w = unit_of(u)
                dve.wait_ge(s_full, UNITS * j + (u + 1))
                dve.sem_inc(tops_begun, 1)
                for t in range(nt):
                    c0, cw = bias_columns(g, n0 + t)
                    last = nc.vector.tensor_tensor_reduce(
                        out=prob[:, u % 2, t * w:(t + 1) * w], in0=sp_[:, u % 2, t * w:(t + 1) * w],
                        in1=bias[:, c0:c0 + cw], scale=slope[:, h:h + 1], scalar=-3e38,
                        op0=ALU.add, op1=ALU.max, accum_out=top[:, u % 4, t:t + 1])
                last.then_inc(s_free, 1)
                dve.wait_ge(s_free, UNITS * j + (u + 3))
                nc.vector.tensor_scalar(ntop[:, u % 4, 0:nt], top[:, u % 4, 0:nt], -1.0, None,
                                        ALU.mult).then_inc(top_ready, 1)

            def copy_t(ev, at, par, j, u):
                dve.wait_ge(t_full, at + 1)
                if ev[0] == "p":
                    dst = probT[:, u % 2, :]
                else:
                    dst = v[ev[1]][:, 4 * ev[2]:4 * ev[2] + 4, :].rearrange("p a c -> p (a c)")
                nc.vector.tensor_copy(dst, tp[:, par, :]).then_inc(t_free, 1)

            def outputs(ch, j, u):
                g, h, n0, nt, w = unit_of(u)
                dve.wait_ge(lnz_ready, UNITS * j + (u + 1))
                ch.link(nc.vector.reciprocal(rz[:, u % 4, 0:nt], z[:, u % 4, 0:nt]))
                dve.wait_ge(o_full, UNITS * j + (u + 1))
                nc.vector.tensor_tensor(o_st[:, 0:nt, HD * h:HD * h + HD],
                                        op[:, u % 2, 0:nt * HD].rearrange("p (t c) -> p t c", t=nt),
                                        bcast(rz[:, u % 4, 0:nt], HD), ALU.mult).then_inc(o_free, 1)
                nc.vector.tensor_tensor(lse[:, 0:nt, HD * h:HD * h + HD],
                                        bcast(top[:, u % 4, 0:nt], HD),
                                        bcast(lnz[:, u % 4, 0:nt], HD), ALU.add).then_inc(o_ready, 1)

            def merge_in(ch, j, e):
                dve.wait_ge(ot_full, NE * j + (e + 1))
                if e < 4:
                    if e == 0:
                        dve.wait_ge(y_done, 4 * j + 1)
                    nc.vector.tensor_copy(tokens(num, e), ot[:, 0:256])
                    nc.vector.tensor_copy(tokens(ref, e), ot[:, 256:512]).then_inc(ot_free, 1)
                    return
                st = stage[:, e % 2]
                if 6 <= e < 10:
                    dve.wait_ge(stage_used, 4 * j + (e - 5))
                else:
                    dve.wait_ge(den_ready, 4 * j + ((e - 5) if e < 6 else (e - 9)) + 2)
                nc.vector.tensor_copy(st.rearrange("p a c -> p (a c)"), ot[:, :]).then_inc(ot_free, 1)
                dve.wait_ge(ot_free, NE * j + (e + 2))
                lb = like(st[:, 1, :], e)
                m = like(mx[:, e % 2, :], e)
                ch.link(nc.vector.tensor_tensor(m, tokens(ref, e), lb, ALU.max))
                ch.link(nc.vector.tensor_tensor(like(ee[:, e % 2, 0, :], e), tokens(ref, e), m,
                                                ALU.subtract))
                nc.vector.tensor_tensor(like(ee[:, e % 2, 1, :], e), lb, m,
                                        ALU.subtract).then_inc(diff_ready, 1)
                if e < 8:
                    ch.link(nc.vector.tensor_copy(tokens(ref, e), m))

            def invert(j, e):
                dve.wait_ge(den_ready, 4 * j + (e - 7) + 2)
                dv = tokens(den, e)
                nc.vector.reciprocal(dv, dv).then_inc(den_inverse, 1)

            dve.sem_inc(s_free, 2)
            dve.sem_inc(t_free, 2)
            dve.sem_inc(o_free, 2)
            dve.sem_inc(ot_free, 1)
            dve.wait_ge(const_in, 64)
            for at in range(T0):
                copy_t(("v", at // 2, at % 2), at, at % 2, 0, 0)
            ch0 = Chain(dve, v_step, 0)
            tops(ch0, 0, 0)
            tops(ch0, 0, 1)
            assert ch0.n == 0

            def step(ch, j, u, table):
                if 1 <= u < UNITS - 1:
                    tops(ch, j, u + 1)
                if u % 2 == 0 and u >= 2:
                    merge_in(ch, j, OT_BY_UNIT[u - 1][0])
                ev = ("p", u)
                copy_t(ev, T0 + NT * j + table[ev], table[ev] % 2, j, u)
                if u == UNITS - 2:
                    merge_in(ch, j, OT_BY_UNIT[u - 1][1])
                outputs(ch, j, u)
                if u in V_AT and ("v", V_AT[u], 0) in table:
                    for half in range(2):
                        ev = ("v", V_AT[u], half)
                        copy_t(ev, T0 + NT * j + table[ev], table[ev] % 2, j, u)

            def pair(ch, j, table, last_pair):
                for u in range(2, UNITS):
                    step(ch, j, u, table)
                invert(j, 8)
                if not last_pair:
                    ch.link(nc.vector.tensor_scalar(slope[:], slope[:], 0.5, None, ALU.mult))
                    tops(ch, j + 1, 0)
                a, b = OT_BY_UNIT[UNITS - 1]
                merge_in(ch, j, a)
                merge_in(ch, j, b)
                if not last_pair:
                    tops(ch, j + 1, 1)
                invert(j, 9)
                if not last_pair:
                    step(ch, j + 1, 0, table)
                invert(j, a)
                if not last_pair:
                    step(ch, j + 1, 1, table)
                invert(j, b)

            STEPS = 41
            for u in range(2):
                step(ch0, 0, u, T_AT)
            with dve.Fori(0, PAIRS - 1) as j:
                ch = Chain(dve, v_step, ch0.n + STEPS * j)
                pair(ch, j, T_AT, False)
                assert ch.n == STEPS, ch.n
            pair(Chain(dve, v_step, ch0.n + STEPS * (PAIRS - 1)), PAIRS - 1, T_LAST, True)


def output_phase(nc, io, keep, layer):
    is_b = layer == 1
    CPM = 2 if is_b else 1
    KO = KT * CPM
    MT = SEQ // P
    BODY = 4
    TURNS = CPM * MT // BODY
    MPB = BODY // CPM
    with ExitStack() as ctx:
        def sb(name, shape, dt=F32):
            return ctx.enter_context(nc.sbuf_tensor(f"{name}_o{layer}", shape, dt))

        def sem(name):
            return ctx.enter_context(nc.semaphore(f"{name}_o{layer}"))

        w_raw = sb("w_raw", [P, 2, D])
        w_hi = sb("w_hi", [P, KO, D], F32R)
        w_lo = sb("w_lo", [P, KO, D], F32R)
        y_hi = sb("y_hi", [P, 2, KT, P], F32R)
        y_lo = sb("y_lo", [P, 2, KT, P], F32R)
        rows = sb("rows", [P, 3, D])
        x_in = sb("x_in", [P, 2, D])
        x_new = sb("x_new", [P, 2, D])
        t = sb("t", [P, D])
        stats = sb("stats", [P, 2, 6])
        mv = sb("mv", [P, 2])
        sd = sb("sd", [P, 3])
        if is_b:
            y_raw = sb("y_raw", [P, 2, KT, P])
            sq = sb("sq", [P, KT, P])
            sqs = sb("sqs", [P, 2, P])
            nw = sb("nw", [P, KO])
            ones = sb("ones", [P, 1])
            rms = sb("rms", [P, 3])
            ps_q = ctx.enter_context(nc.psum_tensor("ps_q", [P, 2, HALF], F32))
        acc = ctx.enter_context(nc.psum_tensor(f"acc_o{layer}", [P, 2, 2, HALF], F32))

        w_in = [sem("w_in0"), sem("w_in1")]
        w_hi_done, w_lo_done = sem("w_hi_done"), sem("w_lo_done")
        rows_in, ones_set = sem("rows_in"), sem("ones_set")
        y_in = [sem("y_in0"), sem("y_in1")]
        x_arr = [sem("x_arr0"), sem("x_arr1")]
        y_ready, y_hi_done, y_lo_done = sem("y_ready"), sem("y_hi_done"), sem("y_lo_done")
        chunk_done, acc_free = sem("chunk_done"), sem("acc_free")
        t_added, var_ready, root_done = sem("t_added"), sem("var_ready"), sem("root_done")
        normed, scaled, out_ready = sem("normed"), sem("scaled"), sem("out_ready")
        out_sent = [sem("out_sent0"), sem("out_sent1")]
        sq_sum, ms_ready, rms_root = sem("sq_sum"), sem("ms_ready"), sem("rms_root")
        stats_whole = sem("stats_whole")
        v_step = sem("v_step")

        block = ctx.enter_context(nc.Block())

        def flat(ap):
            return ap.rearrange("p k c -> p (k c)")

        def in_turns(eng, turn):
            with eng.Fori(0, TURNS - 1) as it:
                turn(it, False)
            turn(TURNS - 1, True)

        def y_tile(g_static, it, c):
            if isinstance(it, int):
                g = BODY * it + c
                return keep["y"][:, :, P * g:P * g + P]
            return keep["y"][:, :, bass.ds(it * (BODY * P) + c * P, P)]

        @block.sync
        def _(sp):
            def load_w(k):
                if k >= 2:
                    sp.wait_ge(w_lo_done, k - 1)
                sp.dma_start(w_raw[:, k % 2, :], io["w_out"][P * k:P * k + P, :]
                             ).then_inc(w_in[k % 2], 16)

            def load_y(m, c):
                k0 = KT * (c % CPM)
                src = io["yT"][m]
                sp.dma_start(y_raw[:, c % 2], src[:, k0:k0 + KT, :]).then_inc(y_in[c % 2], 16)

            if is_b:
                load_y(0, 0)
                load_y(0, 1)
            for k in range(KO):
                load_w(k)
                if k == 1:
                    for m in range(2):
                        sp.dma_start(x_in[:, m, :], io["x_rows"][m]).then_inc(x_arr[m], 16)

            def turn(it, last):
                for c in range(BODY):
                    if is_b and not (last and c >= 2):
                        sp.wait_ge(y_lo_done, BODY * it + (c + 1))
                        load_y(MPB * it + (c + 2) // 2, c)
                    if c % CPM == CPM - 1:
                        s = c // CPM
                        if not (last and s >= MPB - 2):
                            sp.wait_ge(t_added, MPB * it + (s + 1))
                            sp.dma_start(x_in[:, s % 2, :], io["x_rows"][MPB * it + (s + 2)]
                                         ).then_inc(x_arr[s % 2], 16)
                        sp.wait_ge(out_ready, MPB * it + (s + 1))
                        sp.dma_start(io["x_out"][MPB * it + s], x_new[:, s % 2, :]
                                     ).then_inc(out_sent[s % 2], 16)
            in_turns(sp, turn)
            for s in range(2):
                sp.wait_ge(out_sent[s], 16 * (MT // 2 + 1))

        @block.gpsimd
        def _(pool):
            if is_b:
                pool.memset(ones[:], 1.0).then_inc(ones_set, 1)
            for k in range(KO):
                pool.wait_ge(w_hi_done, k + 1)
                nc.gpsimd.tensor_tensor(w_lo[:, k, :], w_raw[:, k % 2, :],
                                        w_hi[:, k, :].bitcast(F32), ALU.subtract).then_inc(w_lo_done, 1)
            pool.wait_ge(rows_in, 16 * (4 if is_b else 3))

            def turn(it, last):
                for s in range(MPB):
                    pool.wait_ge(normed, MPB * it + (s + 2))
                    nc.gpsimd.tensor_tensor(x_new[:, s % 2, :], x_new[:, s % 2, :], rows[:, 1, :],
                                            ALU.mult).then_inc(scaled, 1)
                    pool.wait_ge(scaled, MPB * it + (s + 1))
                    nc.gpsimd.tensor_tensor(x_new[:, s % 2, :], x_new[:, s % 2, :], rows[:, 2, :],
                                            ALU.add).then_inc(out_ready, 1)
            in_turns(pool, turn)

        @block.scalar
        def _(act):
            for n, src in enumerate((io["gate_rows"], io["ln_g"], io["ln_b"])):
                act.dma_start(rows[:, n, :], src[layer].partition_broadcast(P)).then_inc(rows_in, 16)
            if is_b:
                act.dma_start(nw[:], io["norm_w"]).then_inc(rows_in, 16)

            def split_y(it, c):
                g = BODY * it + c
                if is_b:
                    act.wait_ge(y_ready, g + 1)
                    src = y_raw[:, c % 2]
                else:
                    src = y_tile(g, it, c)
                nc.scalar.activation(y_hi[:, c % 2], src, ACT.Copy).then_inc(y_hi_done, 1)

            split_y(0, 0)
            split_y(0, 1)
            for k in range(KO):
                act.wait_ge(w_in[k % 2], 16 * (k // 2 + 1))
                nc.scalar.activation(w_hi[:, k, :], w_raw[:, k % 2, :], ACT.Copy).then_inc(w_hi_done, 1)

            def turn(it, last):
                for c in range(BODY):
                    if not (last and c >= 2):
                        act.wait_ge(chunk_done, BODY * it + (c + 1))
                        if c < 2:
                            split_y(it, c + 2)
                        else:
                            split_y(it + 1, c - 2)
                    if c % CPM == CPM - 1:
                        m = MPB * it + c // CPM
                        if is_b:
                            act.wait_ge(ms_ready, m + 1)
                            nc.scalar.activation(rms[:, 1:2], rms[:, 0:1], ACT.Sqrt).then_inc(rms_root, 1)
                        act.wait_ge(var_ready, m + 1)
                        nc.scalar.activation(sd[:, 1:2], sd[:, 0:1], ACT.Sqrt).then_inc(root_done, 1)
            in_turns(act, turn)

        @block.vector
        def _(dve):
            def prepare(ch, it, c, y_loads):
                g = BODY * it + c
                if is_b:
                    dve.wait_ge(y_in[c % 2], y_loads)
                    src = y_raw[:, c % 2]
                    ch.link(nc.vector.tensor_tensor(sq[:], src, src, ALU.mult))
                    if not (isinstance(it, int) and g < 2):
                        dve.wait_ge(chunk_done, g - 1)
                    nc.vector.tensor_reduce(sqs[:, c % 2, :], sq[:].rearrange("p k c -> p c k"),
                                            AX, ALU.add).then_inc(sq_sum, 1)
                    w0 = KT * (c % CPM)
                    nc.vector.tensor_tensor(src, src, bcast(nw[:, w0:w0 + KT], P),
                                            ALU.mult).then_inc(y_ready, 1)
                else:
                    src = y_tile(g, it, c)
                dve.wait_ge(y_hi_done, g + 1)
                nc.vector.tensor_tensor(y_lo[:, c % 2], src, y_hi[:, c % 2].bitcast(F32),
                                        ALU.subtract).then_inc(y_lo_done, 1)

            def normalise(ch, it, s):
                m = MPB * it + s
                b = s % 2
                dve.wait_ge(chunk_done, CPM * m + CPM)
                if is_b:
                    ch.link(nc.vector.tensor_scalar(rms[:, 0:1], ps_q[:, b, 0:1], 1.0 / (2 * D),
                                                    RMS_EPS, ALU.mult, ALU.add))
                    dve.sem_inc(ms_ready, 1)
                    dve.wait_ge(rms_root, m + 1)
                    ch.link(nc.vector.reciprocal(rms[:, 2:3], rms[:, 1:2]))
                scale = rms[:, 2:3] if is_b else 1.0
                dve.wait_ge(normed, m + 1)
                for n in range(2):
                    ins = nc.vector.scalar_tensor_tensor(
                        t[:, n * HALF:(n + 1) * HALF], acc[:, b, n, :], scale,
                        rows[:, 0, n * HALF:(n + 1) * HALF], ALU.mult, ALU.mult)
                ins.then_inc(acc_free, 1)
                dve.wait_ge(x_arr[b], 16 * (MPB // 2 * it + (s // 2 + 1)))
                dve.wait_ge(acc_free, m + 3)
                nc.vector.scalar_tensor_tensor(t[:], x_in[:, b, :], ALPHA, t[:], ALU.mult,
                                               ALU.add).then_inc(t_added, 1)
                dve.wait_ge(t_added, m + 1)
                nc.vector.bn_stats(stats[:, 0, :], t[:, 0:HALF])
                ch.link(nc.vector.bn_stats(stats[:, 1, :], t[:, HALF:D]))
                dve.sem_inc(stats_whole, 1)
                ch.link(nc.vector.bn_aggr(mv[:], stats[:].rearrange("p a b -> p (a b)")))
                nc.vector.tensor_scalar(sd[:, 0:1], mv[:, 1:2], LN_EPS, None,
                                        ALU.add).then_inc(var_ready, 1)
                dve.wait_ge(root_done, m + 1)
                ch.link(nc.vector.reciprocal(sd[:, 2:3], sd[:, 1:2]))
                dve.wait_ge(out_sent[b], 16 * (MPB // 2 * it + (s // 2 + 1)))
                nc.vector.tensor_scalar(x_new[:, b, :], t[:], mv[:, 0:1], sd[:, 2:3], ALU.subtract,
                                        ALU.mult).then_inc(normed, 1)

            dve.sem_inc(acc_free, 2)
            dve.sem_inc(normed, 1)
            dve.sem_inc(out_sent[0], 16)
            dve.sem_inc(out_sent[1], 16)
            if is_b:
                dve.wait_ge(rows_in, 64)
            ch0 = Chain(dve, v_step, 0)
            prepare(ch0, 0, 0, 16)
            prepare(ch0, 0, 1, 16)
            dve.wait_ge(rows_in, 16 * (4 if is_b else 3))
            steps0 = ch0.n
            steps = 4 + 2 * 5 if is_b else 4 * 3

            def turn(it, last):
                ch = Chain(dve, v_step, steps0 + steps * it)
                for c in range(BODY):
                    if not (last and c >= 2):
                        if c < 2:
                            prepare(ch, it, c + 2, 16 * (2 * it + 2))
                        else:
                            prepare(ch, it + 1, c - 2, 16 * (2 * it + 3))
                    if c % CPM == CPM - 1:
                        normalise(ch, it, c // CPM)
                if not last:
                    assert ch.n == steps, ch.n
            in_turns(dve, turn)

        @block.tensor
        def _(pe):
            if is_b:
                pe.wait_ge(ones_set, 1)

            def turn(it, last, first=False):
                for c in range(BODY):
                    g = BODY * it + c
                    s, b = c // CPM, c // CPM % 2
                    pe.wait_ge(y_lo_done, g + 1)
                    if c % CPM == 0:
                        pe.wait_ge(acc_free, MPB * it + (s + 1))
                    for k in range(KT):
                        kk = KT * (c % CPM) + k
                        if first and c < CPM:
                            pe.wait_ge(w_lo_done, kk + 1)
                        for n, (y, w) in enumerate(((y_hi, w_hi), (y_hi, w_lo), (y_lo, w_hi))):
                            for half in range(2):
                                last_mm = nc.tensor.matmul(
                                    acc[:, b, half, :], y[:, c % 2, k, :],
                                    w[:, kk, half * HALF:(half + 1) * HALF],
                                    start=(kk == 0 and n == 0), stop=(kk == KO - 1 and n == 2))
                    if is_b:
                        pe.wait_ge(sq_sum, g + 1)
                        last_mm = nc.tensor.matmul(ps_q[:, b, 0:1], sqs[:, c % 2, :], ones[:],
                                                   start=(c % CPM == 0), stop=(c % CPM == 1))
                    last_mm.then_inc(chunk_done, 1)
            turn(0, False, True)
            if TURNS > 2:
                with pe.Fori(1, TURNS - 1) as it:
                    turn(it, False)
            turn(TURNS - 1, True)


SSM_INNER = 2 * D
SH = SSM_INNER // HD
NS = 128
GROUPS = 4
GH = SH // GROUPS
TAPS = 5
CH = SEQ // P
XB = 6
SSM_STEPS = 2 * CH
CONV_TILES = GROUPS * XB


def stream_b():
    def xbc(g):
        c0 = SSM_INNER
        return ([c0 + (4 * g + i) * P for i in range(4)] + [c0 + SSM_INNER + g * NS]
                + [c0 + SSM_INNER + (GROUPS + g) * NS])
    order = xbc(0)
    for g in range(GROUPS):
        if g < GROUPS - 1:
            order += xbc(g + 1)
        order += [(4 * g + i) * P for i in range(4)]
    return order


def conv_channels():
    return [c - SSM_INNER for g in range(GROUPS) for c in
            ([SSM_INNER + (4 * g + i) * P for i in range(4)]
             + [2 * SSM_INNER + g * NS, 2 * SSM_INNER + (GROUPS + g) * NS])]


def decay_phase(nc, io, keep):
    with ExitStack() as ctx:
        def sb(name, shape, dt=F32):
            return ctx.enter_context(nc.sbuf_tensor(name, shape, dt))

        def sem(name):
            return ctx.enter_context(nc.semaphore(name))

        W2 = 2 * SH
        x_rows = sb("x_rows", [P, CH, D])
        h_tmp = sb("h_tmp1", [P, 2, HALF])
        ident = sb("ident1", [P, P])
        tri = sb("tri", [P, 3, P])
        wd_raw = sb("wd_raw", [P, KT, W2])
        wd_hi = sb("wd_hi", [P, KT, W2], F32R)
        wd_lo = sb("wd_lo", [P, KT, W2], F32R)
        brow = sb("dt_bias_rows", [P, W2])
        arow = sb("a_rows", [P, W2])
        ac = sb("ac", [P, CH, W2])
        v = sb("sp_v", [P, CH, W2])
        e = sb("sp_e", [P, CH, W2])
        r = sb("sp_r", [P, CH, W2])
        m = sb("sp_m", [P, CH, W2])
        lg = sb("sp_l", [P, CH, W2])
        row_hi = sb("row_hi", [W2, SEQ], F32R)
        row_lo = sb("row_lo", [W2, SEQ], F32R)
        tp = ctx.enter_context(nc.psum_tensor("tp1", [P, 2, HALF], F32))
        dp = ctx.enter_context(nc.psum_tensor("dp", [P, CH, W2], F32))
        cp = ctx.enter_context(nc.psum_tensor("cp", [P, 2, HALF], F32))
        rp = ctx.enter_context(nc.psum_tensor("rp", [P, 2, HALF], F32))

        x_in, const_in = sem("x_in1"), sem("const_in1")
        t_full, h_made, h_hi, h_lo = sem("t_full1"), sem("h_made1"), sem("h_hi1"), sem("h_lo1")
        wd_hi_done, wd_lo_done = sem("wd_hi_done"), sem("wd_lo_done")
        dt_full, neg_abs, exped, logged = sem("dt_full"), sem("neg_abs"), sem("exped"), sem("logged")
        a_done, ac_ready, cum_full, cum_ready = (sem("a_done"), sem("ac_ready"), sem("cum_full"),
                                                 sem("cum_ready"))
        row_full, row_hi_done, row_lo_done, row_out = (sem("row_full"), sem("row_hi_done"),
                                                       sem("row_lo_done"), sem("row_out"))
        v_step = sem("v_step_b1")
        block = ctx.enter_context(nc.Block())

        @block.sync
        def _(sp):
            sp.dma_start(ident[:], io["ident"]).then_inc(const_in, 16)
            sp.dma_start(tri[:], io["tri"]).then_inc(const_in, 16)
            sp.dma_start(wd_raw[:], io["w_dt"]).then_inc(const_in, 16)
            sp.dma_start(brow[:], io["dt_bias"][0].partition_broadcast(P)).then_inc(const_in, 16)
            sp.dma_start(arow[:], io["a_log"][0].partition_broadcast(P)).then_inc(const_in, 16)
            for c in range(CH):
                sp.dma_start(x_rows[:, c, :], io["x_rows"][c]).then_inc(x_in, 16)
            sp.wait_ge(row_hi_done, 2)
            sp.dma_start(io["cum_rows"][0], row_hi[:].bitcast(F32)).then_inc(row_out, 16)
            sp.wait_ge(row_lo_done, 2)
            sp.dma_start(io["cum_rows"][1], row_lo[:].bitcast(F32)).then_inc(row_out, 16)
            sp.wait_ge(row_out, 32)

        @block.tensor
        def _(pe):
            pe.wait_ge(const_in, 80)
            pe.wait_ge(x_in, 16 * CH)
            for n in range(2 * KT):
                if n >= 2:
                    pe.wait_ge(h_made, n - 1)
                for c in range(4):
                    last = nc.tensor.transpose(tp[:, n % 2, c * P:(c + 1) * P],
                                               x_rows[:, 4 * (n % 2) + c, n // 2 * P:n // 2 * P + P],
                                               ident[:])
                last.then_inc(t_full, 1)
            pe.wait_ge(wd_lo_done, 1)
            pe.wait_ge(h_lo, 2 * KT)
            for c in range(CH):
                for k in range(KT):
                    for n, (h, w) in enumerate((("h_hi", wd_hi), ("h_hi", wd_lo), ("h_lo", wd_hi))):
                        last = nc.tensor.matmul(dp[:, c, :], keep[h][:, k, c * P:(c + 1) * P],
                                                w[:, k, :], start=(k == 0 and n == 0),
                                                stop=(k == KT - 1 and n == 2))
            last.then_inc(dt_full, 1)
            pe.wait_ge(ac_ready, 1)
            cum = cp[:, 0, :].rearrange("p (c d h) -> p d c h", c=CH, d=2)
            nc.tensor.matmul(cum[:, 0], tri[:, 0, :], ac[:, :, 0:SH], start=True, stop=True)
            nc.tensor.matmul(cum[:, 1], tri[:, 1, :], ac[:, :, SH:W2], start=True, stop=True)
            nc.tensor.matmul(cp[:, 1, :], tri[:, 2, :], ac[:].rearrange("p c w -> p (c w)"),
                             start=True, stop=True).then_inc(cum_full, 1)
            pe.wait_ge(cum_ready, 1)
            for c in range(CH):
                last = nc.tensor.transpose(rp[0:W2, c // 4, c % 4 * P:(c % 4 + 1) * P],
                                           keep["cum"][:, c, :], ident[:])
            last.then_inc(row_full, 1)

        @block.gpsimd
        def _(pool):
            pool.wait_ge(wd_hi_done, 1)
            nc.gpsimd.tensor_tensor(wd_lo[:], wd_raw[:], wd_hi[:].bitcast(F32),
                                    ALU.subtract).then_inc(wd_lo_done, 1)

        @block.scalar
        def _(act):
            act.wait_ge(const_in, 80)
            nc.scalar.activation(wd_hi[:], wd_raw[:], ACT.Copy).then_inc(wd_hi_done, 1)
            nc.scalar.activation(arow[:], arow[:], ACT.Exp).then_inc(a_done, 1)
            for n in range(2 * KT):
                k = n // 2
                act.wait_ge(t_full, n + 1)
                if n >= 2:
                    act.wait_ge(h_lo, n - 1)
                nc.scalar.activation(h_tmp[:, n % 2, :], tp[:, n % 2, :], ACT.Identity,
                                     bias=keep["mods"][:, 1, k:k + 1],
                                     scale=keep["mods"][:, 1, KT + k:KT + k + 1]).then_inc(h_made, 1)
                act.wait_ge(h_made, n + 1)
                t0 = n % 2 * HALF
                nc.scalar.activation(keep["h_hi"][:, k, t0:t0 + HALF], h_tmp[:, n % 2, :],
                                     ACT.Copy).then_inc(h_hi, 1)
            act.wait_ge(neg_abs, 1)
            nc.scalar.activation(e[:], e[:], ACT.Exp).then_inc(exped, 1)
            act.wait_ge(logged, 1)
            nc.scalar.activation(lg[:], r[:], ACT.Ln).then_inc(exped, 1)
            for n in range(2):
                act.wait_ge(row_full, 1)
                nc.scalar.activation(row_hi[:, n * HALF:(n + 1) * HALF], rp[0:W2, n, :],
                                     ACT.Copy).then_inc(row_hi_done, 1)

        @block.vector
        def _(dve):
            ch = Chain(dve, v_step, 0)
            for n in range(2 * KT):
                k, t0 = n // 2, n % 2 * HALF
                dve.wait_ge(h_hi, n + 1)
                nc.vector.tensor_tensor(keep["h_lo"][:, k, t0:t0 + HALF], h_tmp[:, n % 2, :],
                                        keep["h_hi"][:, k, t0:t0 + HALF].bitcast(F32),
                                        ALU.subtract).then_inc(h_lo, 1)
            dve.wait_ge(dt_full, 1)
            W = [P, CH, W2]
            bb = brow[:].unsqueeze(1).broadcast_to(W)
            ch.link(nc.vector.tensor_tensor(v[:], dp[:], bb, ALU.add))
            ch.link(nc.vector.tensor_scalar(r[:], v[:], -1.0, None, ALU.mult))
            nc.vector.tensor_tensor(e[:], v[:], r[:], ALU.min).then_inc(neg_abs, 1)
            dve.wait_ge(exped, 1)
            nc.vector.tensor_scalar(r[:], e[:], 1.0, None, ALU.add).then_inc(logged, 1)
            dve.wait_ge(logged, 1)
            dve.wait_ge(exped, 2)
            ch.link(nc.vector.tensor_scalar(r[:], r[:], -1.0, None, ALU.add))
            ch.link(nc.vector.tensor_scalar(m[:], r[:], 0.0, None, ALU.is_equal))
            ch.link(nc.vector.tensor_tensor(r[:], r[:], m[:], ALU.add))
            ch.link(nc.vector.reciprocal(r[:], r[:]))
            ch.link(nc.vector.tensor_tensor(m[:], m[:], lg[:], ALU.add))
            ch.link(nc.vector.tensor_tensor(m[:], m[:], e[:], ALU.mult))
            ch.link(nc.vector.tensor_tensor(m[:], m[:], r[:], ALU.mult))
            ch.link(nc.vector.tensor_scalar(v[:], v[:], 0.0, None, ALU.max))
            ch.link(nc.vector.tensor_tensor(keep["dt"][:], v[:], m[:], ALU.add))
            dve.wait_ge(a_done, 1)
            ab = arow[:].unsqueeze(1).broadcast_to(W)
            nc.vector.scalar_tensor_tensor(ac[:], keep["dt"][:], -1.0, ab, ALU.mult,
                                           ALU.mult).then_inc(ac_ready, 1)
            dve.wait_ge(cum_full, 1)
            fl = "p c w -> p (c w)"
            nc.vector.tensor_copy(keep["tot"][:].rearrange(fl), cp[:, 1, :])
            nc.vector.tensor_copy(keep["cum"][:].rearrange(fl), cp[:, 0, :]).then_inc(cum_ready, 1)
            dve.wait_ge(cum_ready, 1)
            nc.vector.tensor_tensor(keep["dif"][:], keep["tot"][:], keep["cum"][:],
                                    ALU.subtract).then_inc(v_step, 1)
            for n in range(2):
                dve.wait_ge(row_hi_done, n + 1)
                nc.vector.tensor_tensor(row_lo[:, n * HALF:(n + 1) * HALF], rp[0:W2, n, :],
                                        row_hi[:, n * HALF:(n + 1) * HALF].bitcast(F32),
                                        ALU.subtract).then_inc(row_lo_done, 1)


def state_space_phase(nc, io, keep):
    with ExitStack() as ctx:
        def sb(name, shape, dt=F32):
            return ctx.enter_context(nc.sbuf_tensor(name, shape, dt))

        def ps(name, shape):
            return ctx.enter_context(nc.psum_tensor(name, shape, F32))

        def sem(name):
            return ctx.enter_context(nc.semaphore(f"{name}_s"))

        GW = GH * HD
        w_raw = sb("w_raw_s", [P, KT, P])
        w_hi = sb("w_hi_s", [P, 2, KT, P], F32R)
        w_lo = sb("w_lo_s", [P, 2, KT, P], F32R)
        stage = sb("stage_s", [P, XB, SEQ])
        pad = sb("pad", [P, SEQ + TAPS - 1])
        th = sb("th", [P, 2, HALF])
        zs = sb("zs", [P, 2, HALF])
        x = sb("x_s", [P, CH, GW])
        cT = sb("cT", [P, SEQ])
        bc = sb("bc", [P, CH, 2, P])
        y = sb("y_s", [P, CH, GW])
        em = sb("em", [P, 2, GH, P])
        xd = sb("xd", [P, 2, GW])
        xw = sb("xw", [P, GW])
        hs = sb("hs", [P, 2, GW])
        hd = sb("hd", [P, GW])
        yt = sb("yt", [P, GW])
        mask_raw = yt[:, 0:2 * P].rearrange("p (a b) -> p a b", a=2)
        yst = sb("yst", [P, 2, HALF])
        crow = sb("crow", [4 * GH, SEQ], F32R)
        sel_raw = sb("sel_raw", [4 * GH, 2 * GH])
        sel = sb("sel", [4 * GH, 2 * GH], F32R)
        mask = sb("mask", [P, 2, P], F32R)
        ident_r = sb("ident_r", [P, P], F32R)
        ident = sb("ident_s", [P, P])
        dskip = sb("dskip", [P, SH])
        conv = sb("conv", [P, GROUPS, XB * (TAPS + 1)])
        gneg, gout, gin, gtot, gdt = (sb(f"g{n}", [P, CH, 2, GH]) for n in
                                      ("neg", "out", "in", "tot", "dt"))
        gd = sb("gd", [P, GH])
        gconv = sb("gconv", [P, XB * (TAPS + 1)])

        pp = ps("pp_s", [P, 2, HALF])
        rows = ps("rows_s", [P, GH, P])
        bc_p = ps("bc_p", [P, 2, P])
        st_p = ps("st_p", [P, GW])
        yo_p = ps("yo_p", [P, GW])
        yd_p = ps("yd_p", [P, GW])
        fill = rows[:].rearrange("p (b h) l -> p b (h l)", b=2)

        names = ("hi_done lo_done pp_full pp_free conv_done tanh_done "
                 "silu_done loc_done sel_done rows_full exp_done "
                 "m_ready xd_ready xw_ready y_set st_full h_ready hd_ready yo_full yd_full "
                 "y_done yf_full y_gated xu_full xu_free c_moved pad_set gconv_done v_step").split()
        S = {n: sem(n) for n in names}
        START = 2
        const_in, w_in, crow_in = sem("const_in"), sem("w_in"), sem("crow_in")
        y_out = [sem("y_out0"), sem("y_out1")]
        block = ctx.enter_context(nc.Block())

        def flat(ap):
            return ap.rearrange("p k c -> p (k c)")


        def wait(eng, name, count):
            eng.wait_ge(S[name], count + START)

        QPS = 3
        UB = 2 * XB

        def unit_step(u):
            return (4 * u + 3) // QPS

        CONV_STEP = {unit_step(2 * f + 1) + 1: f for f in range(XB)}
        EVAC_STEP = {}
        for u in range(UB):
            EVAC_STEP.setdefault(unit_step(u) + 1, []).append(u)
        SPLIT_AT = {0: 1}
        SPLIT_AT.update({unit_step(2 * f - 3) + 1: f for f in range(2, XB + 1)})
        SPLIT_AT.update({SSM_STEPS: XB + 1, 102: XB + 2, 104: XB + 3, 106: XB + 4})
        SPLIT_LAST = {0: 1, 102: 2, 104: 3}
        NU = 14

        def where(s):
            d = s // CH
            return d, (s if d == 0 else 2 * CH - 1 - s)

        def updates(s):
            return 7 * (s // CH) + s % CH

        @block.sync
        def _(sp):
            def load_w(n):
                wait(sp, "lo_done", n)
                sp.dma_start(flat(w_raw[:]), io["b_w"][n]).then_inc(w_in, 16)

            def load_rows(j):
                src = io["cum_rows"].rearrange("a (d h) t -> a d h t", d=2)
                for a in range(2):
                    for d in range(2):
                        r0 = (2 * a + d) * GH
                        sp.dma_start(crow[r0:r0 + GH, :].bitcast(F32),
                                     src[a, d, bass.ds(j * GH, GH), :]).then_inc(crow_in, 16)

            sp.dma_start(flat(w_raw[:]), io["b_w"][0]).then_inc(w_in, 16)
            for dst, src in ((ident[:], io["ident"]), (mask_raw, io["mask"]), (sel_raw[:], io["sel"]),
                             (dskip[:], io["d_skip"][0].partition_broadcast(P)),
                             (conv[:], io["conv"])):
                sp.dma_start(dst, src).then_inc(const_in, 16)
            load_rows(0)
            for n in range(1, XB + 1):
                load_w(n)

            def group(j, last):
                for f in range(1, 4 if last else 10):
                    load_w(10 * j + (XB + f))
                    if f == 7:
                        wait(sp, "rows_full", SSM_STEPS * j + SSM_STEPS)
                        load_rows(j + 1)
                for i in range(8):
                    if i == 5 and not last:
                        load_w(10 * j + (XB + 10))
                    kt, hf = i // 2, i % 2
                    wait(sp, "y_gated", 8 * j + (i + 1))
                    dst = io["yT"][4 * hf:4 * hf + 4, :, bass.ds(4 * j + kt, 1), :]
                    sp.dma_start(dst.rearrange("m p a t -> p m (a t)"),
                                 yst[:, i % 2, :].rearrange("p (m t) -> p m t", m=4)
                                 ).then_inc(y_out[i % 2], 16)

            with sp.Fori(0, GROUPS - 1) as j:
                group(j, False)
            group(GROUPS - 1, True)
            for i in range(2):
                sp.wait_ge(y_out[i], 16 * (4 * GROUPS + 1))

        @block.gpsimd
        def _(pool):
            for n in names:
                pool.sem_inc(S[n], START)
            for o in y_out:
                pool.sem_inc(o, 16)
            pool.memset(pad[:], 0.0).then_inc(S["pad_set"], 1)

            def split_lo(n, slot):
                wait(pool, "hi_done", n + 1)
                nc.gpsimd.tensor_tensor(flat(w_lo[:, slot]), flat(w_raw[:]),
                                        flat(w_hi[:, slot]).bitcast(F32),
                                        ALU.subtract).then_inc(S["lo_done"], 1)

            def per_head(ap):
                return ap.rearrange("p (h c) -> p h c", h=GH)

            def inputs(j, s):
                d, c = where(s)
                if s >= 2:
                    wait(pool, "yd_full", SSM_STEPS * j + (s - 1))
                xv = per_head(x[:, c, :])
                nc.gpsimd.tensor_tensor(per_head(xd[:, s % 2, :]), xv, bcast(gdt[:, c, d, :], HD),
                                        ALU.mult).then_inc(S["xd_ready"], 1)
                if d == 0:
                    nc.gpsimd.tensor_tensor(per_head(y[:, c, :]), xv, bcast(gd[:], HD),
                                            ALU.mult).then_inc(S["y_set"], 1)
                if s % CH < CH - 1:
                    wait(pool, "xd_ready", SSM_STEPS * j + (s + 1))
                    wait(pool, "st_full", NU * j + updates(s))
                    nc.gpsimd.tensor_tensor(per_head(xw[:]), per_head(xd[:, s % 2, :]),
                                            bcast(gin[:, c, d, :], HD),
                                            ALU.mult).then_inc(S["xw_ready"], 1)

            def decayed(j, s):
                if s % CH in (0, CH - 1):
                    return
                d, c = where(s)
                wait(pool, "h_ready", NU * j + updates(s))
                nc.gpsimd.tensor_tensor(per_head(hd[:]), per_head(hs[:, s % 2, :]),
                                        bcast(gtot[:, c, d, :], HD), ALU.mult).then_inc(S["hd_ready"], 1)

            for n in range(XB + 1):
                split_lo(n, n % 2)

            def group(j, last):
                table = SPLIT_LAST if last else SPLIT_AT

                def split(at):
                    if at in table:
                        split_lo(10 * j + (XB + table[at]), table[at] % 2)

                wait(pool, "loc_done", j + 1)
                wait(pool, "xu_free", 8 * j + 8)
                wait(pool, "yf_full", 8 * j)
                inputs(j, 0)
                for s in range(SSM_STEPS):
                    if s + 1 < SSM_STEPS:
                        inputs(j, s + 1)
                    decayed(j, s)
                    split(s)
                split(SSM_STEPS)
                for i in range(8):
                    split(100 + i)
            with pool.Fori(0, GROUPS - 1) as j:
                group(j, False)
            group(GROUPS - 1, True)

        @block.tensor
        def _(pe):
            def project(unit, par, tile, slot, half, part):
                if part == 0:
                    wait(pe, "lo_done", tile + 1)
                    wait(pe, "pp_free", unit - 1)
                for k in (2 * part, 2 * part + 1):
                    for n, (w, h) in enumerate(((w_hi, "h_hi"), (w_hi, "h_lo"), (w_lo, "h_hi"))):
                        last = nc.tensor.matmul(
                            pp[:, par, :], w[:, slot, k, :],
                            keep[h][:, k, half * HALF:(half + 1) * HALF],
                            start=(k == 0 and n == 0), stop=(k == KT - 1 and n == 2))
                if part == 3:
                    last.then_inc(S["pp_full"], 1)

            def begin(j, s):
                d, c = where(s)
                cols = slice(c * P, c * P + P)
                wait(pe, "exp_done", SSM_STEPS * j + s)
                for h in range(GH):
                    if h % 4 == 0:
                        nc.tensor.matmul(rows[:, h:h + 4, :], ident_r[:],
                                         mask[:, d, :].unsqueeze(1).broadcast_to([P, 4, P]),
                                         start=True, stop=False)
                    one = sel[:, GH * d + h:GH * d + h + 1].broadcast_to([4 * GH, P])
                    last = nc.tensor.matmul(rows[:, h, :], one, crow[:, cols], start=False,
                                            stop=(h % 4 == 3))
                last.then_inc(S["rows_full"], 1)

            def states(j, s):
                if s % CH == CH - 1:
                    return
                n, (_, c) = updates(s), where(s)
                wait(pe, "xw_ready", NU * j + (n + 1))
                wait(pe, "h_ready", NU * j + n)
                nc.tensor.matmul(st_p[:], bc[:, c, 1, :], xw[:], start=True,
                                 stop=True).then_inc(S["st_full"], 1)

            def outputs(j, s):
                d, c = where(s)
                wait(pe, "y_done", SSM_STEPS * j + s)
                if s % CH:
                    wait(pe, "h_ready", NU * j + updates(s))
                    nc.tensor.matmul(yo_p[:], cT[:, c * P:(c + 1) * P], hs[:, s % 2, :], start=True,
                                     stop=True)
                wait(pe, "m_ready", SSM_STEPS * j + (s + 1))
                wait(pe, "xd_ready", SSM_STEPS * j + (s + 1))
                for h in range(GH):
                    last = nc.tensor.matmul(yd_p[:, h * HD:(h + 1) * HD], em[:, s % 2, h, :],
                                            xd[:, s % 2, h * HD:(h + 1) * HD], start=True, stop=True)
                last.then_inc(S["yd_full"], 1)

            def unstage(n, i):
                if i == 0:
                    wait(pe, "silu_done", UB * n + UB)
                wait(pe, "xu_free", 8 * n + i)
                for kt in range(4):
                    nc.tensor.transpose(fill[:, 1, kt * P:(kt + 1) * P],
                                        stage[:, kt, i * P:(i + 1) * P], ident[:])
                b, c = (stage[:, f, i * P:(i + 1) * P] for f in (4, 5))
                nc.tensor.matmul(bc_p[:, 0, :], b, c, start=True, stop=True)
                nc.tensor.transpose(bc_p[:, 1, :], b, ident[:]).then_inc(S["xu_full"], 1)

            for u in range(UB):
                for part in range(4):
                    project(u, u % 2, u // 2, u // 2 % 2, u % 2, part)
            pe.wait_ge(const_in, 80)
            for i in range(8):
                unstage(0, i)
            wait(pe, "sel_done", 1)

            def group(j, last):
                units = 20 * j + UB

                def quarter(q):
                    u = q // 4
                    if not last:
                        project(units + u, u % 2, 10 * j + (XB + u // 2), u // 2 % 2, u % 2, q % 4)

                wait(pe, "xu_free", 8 * j + 8)
                wait(pe, "y_gated", 8 * j)
                wait(pe, "c_moved", j + 1)
                pe.wait_ge(crow_in, 64 * j + 64)
                begin(j, 0)
                for s in range(SSM_STEPS):
                    quarter(QPS * s)
                    if s + 1 < SSM_STEPS:
                        begin(j, s + 1)
                    states(j, s)
                    quarter(QPS * s + 1)
                    outputs(j, s)
                    quarter(QPS * s + 2)
                zu = units + (0 if last else UB)
                wait(pe, "exp_done", SSM_STEPS * j + SSM_STEPS)
                for i in range(8):
                    f = i // 2 + (0 if last else XB)
                    tile, slot = 10 * j + (XB + f), f % 2
                    project(zu + i, i % 2, tile, slot, i % 2, 0)
                    project(zu + i, i % 2, tile, slot, i % 2, 1)
                    if i == 0:
                        wait(pe, "y_done", SSM_STEPS * j + SSM_STEPS)
                    wait(pe, "y_gated", 8 * j + i)
                    for c in range(4):
                        last_t = nc.tensor.transpose(
                            fill[:, 0, c * P:(c + 1) * P],
                            y[:, 4 * (i % 2) + c, i // 2 * P:(i // 2 + 1) * P], ident[:])
                    last_t.then_inc(S["yf_full"], 1)
                    if not last and i >= 1:
                        unstage(j + 1, i - 1)
                    project(zu + i, i % 2, tile, slot, i % 2, 2)
                    project(zu + i, i % 2, tile, slot, i % 2, 3)
                if not last:
                    unstage(j + 1, 7)
            with pe.Fori(0, GROUPS - 1) as j:
                group(j, False)
            group(GROUPS - 1, True)

        @block.scalar
        def _(act):
            def put(dst, src, **kw):
                return nc.scalar.activation(dst, src, ACT.Copy, **kw)

            def split_hi(n, slot):
                act.wait_ge(w_in, 16 * n + 16)
                wait(act, "pp_full", 2 * n - 2)
                put(flat(w_hi[:, slot]), flat(w_raw[:])).then_inc(S["hi_done"], 1)

            def to_pad(unit, tile, par, half):
                wait(act, "pp_full", unit + 1)
                if half == 0:
                    wait(act, "conv_done", tile)
                t0 = TAPS // 2 + half * HALF
                put(pad[:, t0:t0 + HALF], pp[:, par, :]).then_inc(S["pp_free"], 1)

            def tanh(tile, f):
                wait(act, "conv_done", tile + 1)
                wait(act, "silu_done", 2 * tile)
                for h in range(2):
                    nc.scalar.activation(th[:, h, :], stage[:, f, h * HALF:(h + 1) * HALF],
                                         ACT.Tanh).then_inc(S["tanh_done"], 1)

            def conv_weights(g):
                src = conv[:, g, :] if isinstance(g, int) else conv[:, bass.ds(g, 1), :].rearrange(
                    "p a c -> p (a c)")
                wait(act, "conv_done", XB * g)
                put(gconv[:], src, scale=0.5).then_inc(S["gconv_done"], 1)

            def factors(j):
                wait(act, "y_done", SSM_STEPS * j)
                cum, dif, tot, dt = (keep[n][:].rearrange("p c (d h) -> p c d h", d=2)
                                     [:, :, :, bass.ds(j * GH, GH)]
                                     for n in ("cum", "dif", "tot", "dt"))
                for d in range(2):
                    put(gneg[:, :, d, :], cum[:, :, d, :], scale=-1.0)
                    put(gdt[:, :, d, :], dt[:, :, d, :])
                    nc.scalar.activation(gout[:, :, d, :], cum[:, :, d, :], ACT.Exp)
                    nc.scalar.activation(gin[:, :, d, :], dif[:, :, d, :], ACT.Exp)
                    nc.scalar.activation(gtot[:, :, d, :], tot[:, :, d, :], ACT.Exp)
                put(gd[:], dskip[:, bass.ds(j * GH, GH)]).then_inc(S["loc_done"], 1)

            def move_c(n):
                wait(act, "silu_done", UB * n + UB)
                wait(act, "y_done", SSM_STEPS * n)
                put(cT[:], stage[:, 5, :]).then_inc(S["c_moved"], 1)

            def unstaged(n, i):
                wait(act, "xu_full", 8 * n + (i + 1))
                if i == 0:
                    wait(act, "y_done", SSM_STEPS * n)
                    wait(act, "xd_ready", SSM_STEPS * n)
                put(x[:, i, :], fill[:, 1, :])
                put(bc[:, i], bc_p[:]).then_inc(S["xu_free"], 1)

            def exponentials(j, s):
                d, c = where(s)
                wait(act, "rows_full", SSM_STEPS * j + (s + 1))
                wait(act, "yd_full", SSM_STEPS * j + (s - 1))
                for h in range(GH):
                    last = nc.scalar.activation(em[:, s % 2, h, :], rows[:, h, :], ACT.Exp,
                                                bias=gneg[:, c, d, h:h + 1])
                last.then_inc(S["exp_done"], 1)

            act.wait_ge(const_in, 80)
            put(ident_r[:], ident[:])
            put(mask[:], mask_raw)
            put(sel[:], sel_raw[:]).then_inc(S["sel_done"], 1)
            conv_weights(0)
            split_hi(0, 0)
            wait(act, "pad_set", 1)
            for f in range(XB):
                n = f + 1
                if n < XB:
                    split_hi(n, n % 2)
                for h in range(2):
                    to_pad(2 * f + h, f, h, h)
                tanh(f, f)
            split_hi(XB, 0)
            for i in range(8):
                unstaged(0, i)
            move_c(0)
            factors(0)

            def group(j, last):
                units = 20 * j + UB
                table = SPLIT_LAST if last else SPLIT_AT

                def split(at):
                    if at in table:
                        split_hi(10 * j + (XB + table[at]), table[at] % 2)

                wait(act, "loc_done", j + 1)
                if not last:
                    conv_weights(j + 1)
                exponentials(j, 0)
                for s in range(SSM_STEPS + 1):
                    if s + 1 < SSM_STEPS:
                        exponentials(j, s + 1)
                    if not last:
                        for u in EVAC_STEP.get(s, ()):
                            to_pad(units + u, XB * j + (XB + u // 2), u % 2, u % 2)
                    split(s)
                    if not last and s - 1 in CONV_STEP:
                        f = CONV_STEP[s - 1]
                        tanh(XB * j + (XB + f), f)
                if not last:
                    tanh(XB * j + (XB + 5), 5)
                    wait(act, "silu_done", UB * j + 2 * UB)
                zu = units + (0 if last else UB)
                for i in range(8):
                    split(100 + i)
                    if not last and i == 0:
                        factors(j + 1)
                    if not last and i >= 1:
                        unstaged(j + 1, i - 1)
                    wait(act, "pp_full", zu + (i + 1))
                    wait(act, "y_gated", 8 * j + (i - 1 if i >= 2 else 0))
                    nc.scalar.activation(th[:, i % 2, :], pp[:, i % 2, :], ACT.Tanh, scale=0.5)
                    put(zs[:, i % 2, :], pp[:, i % 2, :], scale=0.5).then_inc(S["pp_free"], 1)
                if not last:
                    unstaged(j + 1, 7)
                    move_c(j + 1)
            with act.Fori(0, GROUPS - 1) as j:
                group(j, False)
            group(GROUPS - 1, True)

        @block.vector
        def _(dve):
            def per_head(ap):
                return ap.rearrange("p (h c) -> p h c", h=GH)

            def weigh(ch, j, s):
                _, c = where(s)
                wait(dve, "exp_done", SSM_STEPS * j + (s + 1))
                nc.vector.tensor_tensor(em[:, s % 2], em[:, s % 2],
                                        bc[:, c, 0, :].unsqueeze(1).broadcast_to([P, GH, P]),
                                        ALU.mult).then_inc(S["m_ready"], 1)

            def update(ch, j, s):
                if s % CH == CH - 1:
                    return
                n = updates(s)
                wait(dve, "st_full", NU * j + (n + 1))
                if s % CH == 0:
                    nc.vector.tensor_copy(hs[:, (s + 1) % 2, :], st_p[:]).then_inc(S["h_ready"], 1)
                else:
                    wait(dve, "hd_ready", 12 * j + (6 * (s // CH) + s % CH))
                    nc.vector.tensor_tensor(hs[:, (s + 1) % 2, :], hd[:], st_p[:],
                                            ALU.add).then_inc(S["h_ready"], 1)

            def assemble(ch, j, s):
                d, c = where(s)
                wait(dve, "yd_full", SSM_STEPS * j + (s + 1))
                wait(dve, "y_set", 8 * j + (s + 1 if d == 0 else 8))
                if s % CH == 0:
                    nc.vector.tensor_tensor(y[:, c, :], y[:, c, :], yd_p[:],
                                            ALU.add).then_inc(S["y_done"], 1)
                else:
                    ch.link(nc.vector.tensor_tensor(per_head(yt[:]), per_head(yo_p[:]),
                                                    bcast(gout[:, c, d, :], HD), ALU.mult))
                    ch.link(nc.vector.tensor_tensor(yt[:], yt[:], yd_p[:], ALU.add))
                    nc.vector.tensor_tensor(y[:, c, :], y[:, c, :], yt[:],
                                            ALU.add).then_inc(S["y_done"], 1)
                wait(dve, "y_done", SSM_STEPS * j + (s + 1))

            def convolve(ch, tile, unit, f, k0=0, k1=TAPS):
                w = gconv[:, (TAPS + 1) * f:(TAPS + 1) * (f + 1)]
                out = stage[:, f, :]
                for k in range(k0, k1):
                    if k == 0:
                        wait(dve, "pp_free", unit + 1)
                        ins = nc.vector.tensor_scalar(out, pad[:, 0:SEQ], w[:, 0:1],
                                                      w[:, TAPS:TAPS + 1], ALU.mult, ALU.add)
                    else:
                        ins = nc.vector.scalar_tensor_tensor(out, pad[:, k:k + SEQ], w[:, k:k + 1],
                                                             out, ALU.mult, ALU.add)
                    if k < TAPS - 1:
                        ch.link(ins)
                    else:
                        ins.then_inc(S["conv_done"], 1)

            def silu(tile, f):
                for h in range(2):
                    wait(dve, "tanh_done", 2 * tile + (h + 1))
                    v = stage[:, f, h * HALF:(h + 1) * HALF]
                    nc.vector.scalar_tensor_tensor(v, th[:, h, :], 1.0, v, ALU.add,
                                                   ALU.mult).then_inc(S["silu_done"], 1)

            dve.wait_ge(const_in, 80)
            wait(dve, "pad_set", 1)
            wait(dve, "gconv_done", 1)
            ch0 = Chain(dve, S["v_step"], START)
            for f in range(XB):
                convolve(ch0, f, 2 * f + 1, f)
                silu(f, f)
            steps0 = ch0.n
            STEPS = 28 + 4 * XB + 8

            def group(j, last):
                ch = Chain(dve, S["v_step"], START + steps0 + STEPS * j)
                units = 20 * j + UB
                wait(dve, "loc_done", j + 1)
                wait(dve, "xu_free", 8 * j + 8)
                weigh(ch, j, 0)
                if not last:
                    wait(dve, "gconv_done", j + 2)
                    wait(dve, "xu_full", 8 * j + 8)
                    wait(dve, "c_moved", j + 1)
                for s in range(SSM_STEPS):
                    update(ch, j, s)
                    if not last and s - 1 in CONV_STEP:
                        f = CONV_STEP[s - 1]
                        convolve(ch, XB * j + (XB + f), units + 2 * f + 1, f, 2, TAPS)
                    if s + 1 < SSM_STEPS:
                        weigh(ch, j, s + 1)
                    assemble(ch, j, s)
                    if not last:
                        if s in CONV_STEP:
                            f = CONV_STEP[s]
                            convolve(ch, XB * j + (XB + f), units + 2 * f + 1, f, 0, 2)
                        if s - 1 in CONV_STEP:
                            f = CONV_STEP[s - 1]
                            silu(XB * j + (XB + f), f)
                if not last:
                    convolve(ch, XB * j + (XB + 5), units + 11, 5)
                    silu(XB * j + (XB + 5), 5)
                zu = units + (0 if last else UB)
                for i in range(8):
                    wait(dve, "pp_free", zu + (i + 1))
                    ch.link(nc.vector.scalar_tensor_tensor(zs[:, i % 2, :], th[:, i % 2, :], 1.0,
                                                           zs[:, i % 2, :], ALU.add, ALU.mult))
                    wait(dve, "yf_full", 8 * j + (i + 1))
                    dve.wait_ge(y_out[i % 2], 64 * j + 16 * (i // 2 + 1))
                    nc.vector.tensor_tensor(yst[:, i % 2, :], fill[:, 0, :], zs[:, i % 2, :],
                                            ALU.mult).then_inc(S["y_gated"], 1)
                if not last:
                    assert ch.n == STEPS, ch.n
            with dve.Fori(0, GROUPS - 1) as j:
                group(j, False)
            group(GROUPS - 1, True)


def build(nc, io, out):
    def scratch(name, shape):
        return nc.dram_tensor(name, shape, F32, kind="Internal").ap()

    io["gate_rows"] = scratch("gate_rows", (DEPTH, D))
    io["x1"] = scratch("x1", (SEQ // P, P, D))
    io["cum_rows"] = scratch("cum_rows", (2, 2 * SH, SEQ))
    io["yT"] = scratch("yT_b", (SEQ // P, P, 2 * KT, P))
    with ExitStack() as ctx:
        keep = {"mods": ctx.enter_context(nc.sbuf_tensor("mods", [P, DEPTH, 2 * KT], F32))}

        def split_h(scope, layer):
            for n in ("h_hi", "h_lo"):
                keep[n] = scope.enter_context(nc.sbuf_tensor(f"{n}{layer}", [P, KT, SEQ], F32R))

        with ExitStack() as layer_a:
            keep["y"] = layer_a.enter_context(nc.sbuf_tensor("yT", [P, PAIRS, SEQ], F32))
            with ExitStack() as scope:
                split_h(scope, 0)
                modulation_phase(nc, io, keep)
                with nc.cleanup_on_exit():
                    attention_phase(nc, io, keep)
            io["x_rows"], io["x_out"], io["w_out"] = io["x"], io["x1"], io["a_w_out"]
            output_phase(nc, io, keep, 0)
        io["x_rows"] = io["x1"]
        with ExitStack() as scope:
            split_h(scope, 1)
            for n in ("cum", "dif", "tot", "dt"):
                keep[n] = scope.enter_context(nc.sbuf_tensor(f"all_{n}", [P, CH, 2 * SH], F32))
            decay_phase(nc, io, keep)
            state_space_phase(nc, io, keep)
        io["x_out"], io["w_out"] = out, io["b_w_out"]
        output_phase(nc, io, keep, 1)


def kernel(**inputs):
    import numpy as _np
    import concourse.bacc as _bacc
    from concourse.bass_utils import run_bass_kernel_spmd as _run

    nc = _bacc.Bacc("TRN2", target_bir_lowering=False, num_devices=1)
    arrays, io = {}, {}

    def given(name, a):
        a = _np.ascontiguousarray(a)
        arrays[f"in_{name}"] = a
        io[name] = nc.dram_tensor(f"in_{name}", a.shape, F32, kind="ExternalInput").ap()

    def tiles(w, cols, width=P):
        k = w.shape[0] // P
        w = w.reshape(k, P, w.shape[1])
        return _np.stack([w[:, :, c:c + width].transpose(1, 0, 2) for c in cols])

    g = {n: _np.asarray(v) for n, v in inputs.items()}
    x = g["x"][0]
    given("x", x.reshape(SEQ // P, P, D))
    given("xT", x.T.reshape(KT, P, SEQ).transpose(1, 0, 2))
    given("c", g["c"].reshape(KT, P).T)
    given("ada_w", g["ada_w"])
    given("ada_b", g["ada_b"][None])
    given("ln_g", g["ln_g"])
    given("ln_b", g["ln_b"])
    given("a_w", tiles(g["a_w_in"][0], stream_a()))
    given("a_w_out", g["a_w_out"][0])

    given("b_w", tiles(g["b_w_in"][0], stream_b()).reshape(10 * GROUPS, P, KT * P))
    given("w_dt", tiles(g["b_w_in"][0], [2 * SSM_INNER + 2 * GROUPS * NS],
                        2 * SH)[0])
    given("b_w_out", g["b_w_out"][0])
    given("dt_bias", g["b_dt_bias"].reshape(1, 2 * SH))
    given("a_log", g["b_a_log"].reshape(1, 2 * SH))
    given("d_skip", g["b_d"])
    given("norm_w", g["b_norm_w"][0].reshape(2 * KT, P).T)
    cw = _np.concatenate([g["b_conv_w"][0], g["b_conv_b"]], 0)
    cw = _np.stack([cw[:, c:c + P] for c in conv_channels()])
    given("conv", cw.transpose(2, 0, 1).reshape(P, GROUPS, XB * (TAPS + 1)))
    s, t = _np.arange(P)[:, None], _np.arange(P)[None, :]
    given("tri", _np.stack([s <= t, s >= t, s == s + 0 * t], 1).astype(_np.float32))
    given("mask", _np.stack([_np.where(t >= s, 0.0, MASKED), _np.where(t <= s, 0.0, MASKED)],
                            1).astype(_np.float32))
    given("sel", _np.tile(_np.eye(2 * GH, dtype=_np.float32), (2, 1)))

    slope = 2.0 ** (-8.0 * (_np.arange(2, dtype=_np.float32) + 1.0) / HEADS)
    rows = _np.repeat(slope, HD)[:, None]
    given("bias", bias_tables())
    given("ident", _np.eye(P, dtype=_np.float32))
    given("slope", _np.tile(slope[None, :], (P, 1)).astype(_np.float32))
    given("qscale", _np.concatenate([1 / (8 * rows), 2 / (8 * rows)], 1).astype(_np.float32))

    out = nc.dram_tensor("out", (SEQ // P, P, D), F32, kind="ExternalOutput").ap()
    build(nc, io, out)
    r = _run(nc, [arrays], core_ids=[0])
    return _np.asarray(r.results[0]["out"]).reshape(1, SEQ, D)
```

```python
from contextlib import ExitStack

import concourse.bass as bass
from concourse import mybir

F32 = mybir.dt.float32
F32R = mybir.dt.float32r
ALU = mybir.AluOpType
ACT = mybir.ActivationFunctionType

P = 128
SEQ = 1024
D = 1024
KT = D // P
HALF = 512
DEPTH = 2
ALPHA = (2 * DEPTH) ** 0.25
LN_EPS = 1e-5
RMS_EPS = 1e-5

HEADS, HD = 16, 64
PAIRS = HEADS // 2
DILS = (1, 4, 16)
RADIUS = 64
MASKED = -2.0 ** 100
KC0 = SEQ + 2 * RADIUS
VT2, Q2, K2, VT0, Q0, K0, GATE, VT1, Q1, K1 = range(10)
FIRST_TILES = (VT0, Q0, K0, VT1, Q1, K1)
LAST_TILES = (VT2, Q2, K2, GATE)
TILE_GROUP = {VT2: (2, 2), Q2: (2, 0), K2: (2, 1), VT0: (0, 2), Q0: (0, 0), K0: (0, 1),
              VT1: (1, 2), Q1: (1, 0), K1: (1, 1)}
UNITS = 20

def stream_a():
    def col(kind, pair):
        if kind == GATE:
            return 9 * D + pair * P
        g, which = TILE_GROUP[kind]
        return (3 * g + which) * D + pair * P
    order = [col(k, 0) for k in FIRST_TILES]
    for j in range(PAIRS):
        if j < PAIRS - 1:
            order += [col(k, j + (k in FIRST_TILES)) for k in range(10)]
        else:
            order += [col(k, j) for k in LAST_TILES]
    return order

def unit_of(u):
    if u < 16:
        return u // 8, u % 2, 2 * (u % 8 // 2), 2, 256
    return 2, u % 2, 4 * ((u - 16) // 2), 4, 128

def bias_tables():
    import numpy as np
    q = np.arange(P)[:, None]
    c = np.arange(256)[None, :]
    out = []
    for first, last in ((True, False), (False, False), (False, True)):
        d = np.abs(c - RADIUS - q)
        ok = (d <= RADIUS) & (c >= RADIUS * first) & (c < 256 - RADIUS * last)
        out.append(np.where(ok, -d, MASKED))
    wide = np.arange(384)[None, :]
    d = np.abs(wide - P - q)
    out.append(np.where(d <= RADIUS, -4.0 * d, MASKED))
    c = np.arange(P)[None, :]
    out.append(np.where(q // 64 == c // 64, -16.0 * np.abs(q % 64 - c % 64), MASKED))
    return np.concatenate(out, 1).astype(np.float32)

def bias_columns(g, n):
    if g == 0:
        return 256 * (0 if n == 0 else 2 if n == 7 else 1), 256
    if g == 1:
        return 768 + P * (1 - n % 2), 256
    return 1152, P

class Chain:

    def __init__(self, eng, sem, base):
        self.eng, self.sem, self.base, self.n = eng, sem, base, 0

    def link(self, ins):
        self.n += 1
        ins.then_inc(self.sem, 1)
        self.eng.wait_ge(self.sem, self.base + self.n)

def bcast(ap, n):
    return ap.unsqueeze(len(ap.shape)).broadcast_to(list(ap.shape) + [n])

def modulation_products(nc, acc, brow, ones, ps_col, ps_gate, col_full, gate_full):
    for n in range(2 * KT):
        last = nc.tensor.matmul(ps_col[:, n:n + 1], acc[:, n * P:(n + 1) * P], ones[:, 0:1],
                                start=True, stop=True)
    last.then_inc(col_full, 1)
    for n in range(2):
        c0 = 2 * D + n * HALF
        nc.tensor.matmul(ps_gate[:, n, :], ones[:], acc[:, c0:c0 + HALF], start=True, stop=False)
        last = nc.tensor.matmul(ps_gate[:, n, :], ones[0:1, :], brow[0:1, n * HALF:(n + 1) * HALF],
                                start=False, stop=True)
    last.then_inc(gate_full, 1)

def modulation_phase(nc, io, keep):
    with ExitStack() as ctx:
        def sb(name, shape, dt=F32):
            return ctx.enter_context(nc.sbuf_tensor(name, shape, dt))

        def sem(name):
            return ctx.enter_context(nc.semaphore(name))

        RING, XR, HR = 3, 3, 4
        w_ring = sb("ada_ring", [P, RING, 3 * D])
        acc = sb("ada_acc", [P, 3 * D])
        cc = sb("c_cols", [P, 3, KT])
        brow = sb("ada_b_row", [1, D])
        bcol = sb("ada_b_cols", [P, 2 * KT])
        ones = sb("ones", [P, P])
        gate_sb = sb("gate_sb", [1, D])
        x_ring = sb("xT_ring", [P, XR, SEQ])
        h_tmp = sb("h_tmp", [P, HR, SEQ])
        ps_col = ctx.enter_context(nc.psum_tensor("ps_col", [P, HALF], F32))
        ps_gate = ctx.enter_context(nc.psum_tensor("ps_gate", [P, 2, HALF], F32))
        cond, mods = keep["cond"], keep["mods"]

        c_in, b_in, c_exp = sem("c_in"), sem("b_in"), sem("c_exp")
        ones_set = sem("ones_set")
        w_in = [sem(f"ada_in{i}") for i in range(RING)]
        w_used = sem("ada_used")
        col_full, mods_ready, gate_full = sem("col_full"), sem("mods_ready"), sem("gate_full")
        gate_copied, gate_out = sem("gate_copied"), sem("gate_out")
        x_in = [sem(f"xT_in{i}") for i in range(XR)]
        h_made, h_hi, h_lo = sem("h_made"), sem("h_hi"), [sem("h_lo0"), sem("h_lo1")]
        tile_in, tile_hi, ident_in = sem("tile_in"), sem("tile_hi"), sem("ident_in")
        v_step = sem("v_step")
        block = ctx.enter_context(nc.Block())

        @block.sync
        def _(sp):
            sp.dma_start(cc[:, 0, :], io["c"]).then_inc(c_in, 16)
            for k in range(KT):
                if k >= RING:
                    sp.wait_ge(w_used, k - RING + 1)
                sp.dma_start(w_ring[:, k % RING, :], io["ada_w"][0, P * k:P * k + P, :]
                             ).then_inc(w_in[k % RING], 16)
                if k == 0:
                    sp.dma_start(brow[:], io["ada_b"][:, 0, 2 * D:3 * D]).then_inc(b_in, 16)
                    sp.dma_start(bcol[:], io["ada_b_cols"][0]).then_inc(b_in, 16)
                if k == KT - 2:
                    for n in range(2):
                        sp.dma_start(keep["w_raw"][:, n], io["a_w"][n]).then_inc(tile_in, 16)
            for k in range(XR):
                sp.dma_start(x_ring[:, k, :], io["xT"][:, k, :]).then_inc(x_in[k], 16)
            sp.dma_start(keep["ident"][:], io["ident"]).then_inc(ident_in, 16)
            sp.wait_ge(ident_in, 16)

        @block.gpsimd
        def _(pool):
            pool.memset(ones[:], 1.0).then_inc(ones_set, 1)
            for n in range(2):
                pool.wait_ge(tile_hi, n + 1)
                nc.gpsimd.tensor_tensor(keep["w_lo"][:, n], keep["w_raw"][:, n],
                                        keep["w_hi"][:, n].bitcast(F32), ALU.subtract)
            for k in range(1, KT, 2):
                pool.wait_ge(h_hi, k + 1)
                nc.gpsimd.tensor_tensor(keep["h_lo"][:, k, :], h_tmp[:, k % HR, :],
                                        keep["h_hi"][:, k, :].bitcast(F32),
                                        ALU.subtract).then_inc(h_lo[1], 1)

        @block.scalar
        def _(act):
            act.wait_ge(c_in, 16)
            nc.scalar.activation(cc[:, 1, :], cc[:, 0, :], ACT.Exp, scale=-1.0).then_inc(c_exp, 1)
            act.wait_ge(tile_in, 32)
            for n in range(2):
                nc.scalar.activation(keep["w_hi"][:, n], keep["w_raw"][:, n],
                                     ACT.Copy).then_inc(tile_hi, 1)
            for k in range(KT):
                act.wait_ge(h_made, k + 1)
                nc.scalar.activation(keep["h_hi"][:, k, :], h_tmp[:, k % HR, :],
                                     ACT.Copy).then_inc(h_hi, 1)
                if k + XR < KT:
                    act.dma_start(x_ring[:, k % XR, :], io["xT"][:, k + XR, :]
                                  ).then_inc(x_in[k % XR], 16)
            act.wait_ge(gate_copied, 1)
            act.dma_start(io["gate_row"][0:1, :], gate_sb[:]).then_inc(gate_out, 16)
            act.wait_ge(gate_out, 16)

        @block.vector
        def _(dve):
            ch = Chain(dve, v_step, 0)
            dve.wait_ge(c_exp, 1)
            ch.link(nc.vector.tensor_scalar(cc[:, 2, :], cc[:, 1, :], 1.0, None, ALU.add))
            ch.link(nc.vector.reciprocal(cc[:, 1, :], cc[:, 2, :]))
            ch.link(nc.vector.tensor_tensor(cond[:], cc[:, 0, :], cc[:, 1, :], ALU.mult))
            for k in range(KT):
                dve.wait_ge(w_in[k % RING], 16 * (k // RING + 1))
                if k == 0:
                    ins = nc.vector.tensor_scalar(acc[:], w_ring[:, k % RING, :],
                                                  cond[:, k:k + 1], None, ALU.mult)
                else:
                    dve.wait_ge(w_used, k)
                    ins = nc.vector.scalar_tensor_tensor(acc[:], w_ring[:, k % RING, :],
                                                         cond[:, k:k + 1], acc[:], ALU.mult, ALU.add)
                ins.then_inc(w_used, 1)
            dve.wait_ge(col_full, 1)
            dve.wait_ge(b_in, 32)
            ch.link(nc.vector.tensor_tensor(mods[:, 0, :], ps_col[:, 0:2 * KT], bcol[:], ALU.add))
            nc.vector.tensor_scalar(mods[:, 0, KT:2 * KT], mods[:, 0, KT:2 * KT], 1.0, None,
                                    ALU.add).then_inc(mods_ready, 1)
            dve.wait_ge(mods_ready, 1)
            def rest_of_h(k):
                dve.wait_ge(h_hi, k + 1)
                nc.vector.tensor_tensor(keep["h_lo"][:, k, :], h_tmp[:, k % HR, :],
                                        keep["h_hi"][:, k, :].bitcast(F32),
                                        ALU.subtract).then_inc(h_lo[0], 1)

            for k in range(KT):
                dve.wait_ge(x_in[k % XR], 16 * (k // XR + 1))
                if k >= HR:
                    dve.wait_ge(h_lo[k % 2], (k - HR) // 2 + 1)
                nc.vector.tensor_scalar(h_tmp[:, k % HR, :], x_ring[:, k % XR, :],
                                        mods[:, 0, KT + k:KT + k + 1], mods[:, 0, k:k + 1],
                                        ALU.mult, ALU.add).then_inc(h_made, 1)
                if k % 2:
                    rest_of_h(k - 1)
            dve.wait_ge(gate_full, 1)
            nc.vector.tensor_copy(gate_sb[:], ps_gate[0:1, :, :].rearrange("p a b -> p (a b)")
                                  ).then_inc(gate_copied, 1)

        @block.tensor
        def _(pe):
            pe.wait_ge(ones_set, 1)
            pe.wait_ge(b_in, 32)
            pe.wait_ge(w_used, KT)
            modulation_products(nc, acc, brow, ones, ps_col, ps_gate, col_full, gate_full)

def attention_phase(nc, io, keep):
    with ExitStack() as ctx:
        def sb(name, shape, dt=F32):
            return ctx.enter_context(nc.sbuf_tensor(name, shape, dt))

        def ps(name, shape):
            return ctx.enter_context(nc.psum_tensor(name, shape, F32))

        def sem(name):
            return nc.alloc_semaphore(name)

        w_raw, w_hi, w_lo, ident = (keep[n] for n in ("w_raw", "w_hi", "w_lo", "ident"))
        qT = [sb(f"qT{g}", [P, SEQ]) for g in range(3)]
        kT = [sb(f"kT{g}", [P, KC0 if g == 0 else SEQ]) for g in range(3)]
        vT = sb("vT", [P, SEQ])
        v = [sb(f"v{g}", [P, 8, P]) for g in range(3)]
        gate = sb("gate", [P, SEQ])
        bias = sb("bias", [P, 1280])
        slope = sb("slope", [P, 2])
        qscale = sb("qscale", [P, 2])
        prob = sb("prob", [P, 2, HALF])
        probT = sb("probT", [P, 2, HALF])
        top = sb("top", [P, 4, 4])
        ntop = sb("ntop", [P, 4, 4])
        z = sb("z", [P, 4, 4])
        rz = sb("rz", [P, 4, 4])
        lnz = sb("lnz", [P, 4, 4])
        o_st = sb("o_st", [P, 4, P])
        lse = sb("lse", [P, 4, P])
        stage = sb("stage", [P, 2, 2, 256])
        num = sb("num", [P, SEQ])
        den = sb("den", [P, SEQ])
        ref = sb("ref", [P, SEQ])
        ee = sb("ee", [P, 2, 2, 256])
        mx = sb("mx", [P, 2, 256])

        pp = ps("pp", [P, 2, HALF])
        sp_ = ps("sp_", [P, 2, HALF])
        tp = ps("tp", [P, 2, HALF])
        op = ps("op", [P, 2, 256])
        ot = ps("ot", [P, HALF])

        const_in = sem("const_in")
        w_in = [sem("w_in0"), sem("w_in1")]
        hi_done, lo_done = sem("hi_done"), sem("lo_done")
        pp_full, pp_free = sem("pp_full"), sem("pp_free")
        s_full, s_free = sem("s_full"), sem("s_free")
        tops_begun = sem("tops_begun")
        top_ready, p_ready, lnz_ready = sem("top_ready"), sem("p_ready"), sem("lnz_ready")
        t_full, t_free = sem("t_full"), sem("t_free")
        o_full, o_free, o_ready = sem("o_full"), sem("o_free"), sem("o_ready")
        ot_full, ot_free = sem("ot_full"), sem("ot_free")
        diff_ready, wt_ready, stage_used = sem("diff_ready"), sem("wt_ready"), sem("stage_used")
        den_ready, den_inverse, y_done = sem("den_ready"), sem("den_inverse"), sem("y_done")
        g_step, y_begun = sem("g_step"), sem("y_begun")
        scale_set = sem("scale_set")
        v_step = sem("v_step1")

        V_AT = {3: 2, 9: 0, 17: 1}

        def t_events(steps=UNITS, v_at=V_AT):
            out = []
            for u in range(steps):
                out.append(("p", u))
                if u in v_at:
                    out += [("v", v_at[u], 0), ("v", v_at[u], 1)]
            return out

        T_EVENTS = t_events()
        NT = len(T_EVENTS)
        T_AT = {e: n for n, e in enumerate(T_EVENTS)}
        T_LAST = {e: n for n, e in enumerate(t_events(v_at={3: 2}))}
        T0 = 4
        OT_BY_UNIT = {u: ([u // 2] if u < 16 else [8 + (u - 17), 9 + (u - 17)])
                      for u in range(1, UNITS, 2)}
        NE = 12
        STEP_TILES = tuple(range(10))

        def tokens(buf, e):
            if e < 4:
                return buf[:, 256 * e:256 * e + 256]
            if e < 8:
                return buf[:, :].rearrange("p (i r) -> p r i", r=4)[:, e - 4, :]
            m = e - 8
            return buf[:, :].rearrange("p (i r) -> p r i", r=16)[:, 4 * m:4 * m + 4, :]

        def like(flat, e):
            return flat if e < 8 else flat.rearrange("p (r i) -> p r i", r=4)

        block = ctx.enter_context(nc.Block())

        @block.sync
        def _(sp):
            def load(n, slot):
                sp.dma_start(w_raw[:, slot], io["a_w"][n]).then_inc(w_in[slot], 16)

            for slot in range(2):
                sp.sem_inc(w_in[slot], 16)
            sp.dma_start(bias[:], io["bias"]).then_inc(const_in, 16)
            sp.dma_start(slope[:], io["slope"]).then_inc(const_in, 16)
            sp.dma_start(qscale[:], io["qscale"]).then_inc(const_in, 16)
            for n in range(2, 6):
                sp.wait_ge(lo_done, n - 1)
                load(n, n % 2)
            with sp.Fori(0, PAIRS - 1) as j:
                for f in range(10):
                    sp.wait_ge(lo_done, 10 * j + (6 + f - 1))
                    load(10 * j + (6 + f), f % 2)
            for f in range(4):
                n = 10 * (PAIRS - 1) + 6 + f
                sp.wait_ge(lo_done, n - 1)
                load(n, f % 2)

        @block.gpsimd
        def _(pool):
            def split_lo(n, slot):
                pool.wait_ge(hi_done, n + 1)
                nc.gpsimd.tensor_tensor(w_lo[:, slot].rearrange("p k c -> p (k c)"),
                                        w_raw[:, slot].rearrange("p k c -> p (k c)"),
                                        w_hi[:, slot].rearrange("p k c -> p (k c)").bitcast(F32),
                                        ALU.subtract).then_inc(lo_done, 1)
            def merge(ch, j, e):
                if e == 8:
                    pool.wait_ge(stage_used, 4 * j + 4)
                pool.wait_ge(wt_ready, 8 * j + (e - 3))
                e0, e1 = (like(ee[:, e % 2, i, :], e) for i in range(2))
                st, g = like(stage[:, e % 2, 0, :], e), like(mx[:, e % 2, :], e)
                nv, dv = tokens(num, e), tokens(den, e)
                nc.gpsimd.tensor_tensor(nv, nv, e0, ALU.mult)
                ch.link(nc.gpsimd.tensor_tensor(st, st, e1, ALU.mult))
                if e < 8:
                    nc.gpsimd.tensor_tensor(dv, e0, e1, ALU.add)
                    nc.gpsimd.tensor_tensor(nv, nv, st, ALU.add).then_inc(stage_used, 1)
                    return
                nc.gpsimd.tensor_tensor(nv, nv, st, ALU.add)
                ch.link(nc.gpsimd.tensor_tensor(dv, dv, e0, ALU.mult))
                nc.gpsimd.tensor_tensor(nv, nv, tokens(gate, e), ALU.mult)
                ch.link(nc.gpsimd.tensor_tensor(dv, dv, e1, ALU.add))
                ch.link(nc.gpsimd.tensor_tensor(g, g, dv, ALU.mult))
                nc.gpsimd.tensor_tensor(dv, dv, g, ALU.add).then_inc(den_ready, 1)

            def gated(j, e):
                pool.wait_ge(den_inverse, 4 * j + (e - 7))
                pool.sem_inc(y_begun, 1)
                m = e - 8
                y = keep["trunk"][:].rearrange("p (m k i r) -> p k r m i", k=PAIRS, m=SEQ // P, r=16)
                y = y[:, j] if isinstance(j, int) else y[:, bass.ds(j, 1)].rearrange(
                    "p a r m i -> p (a r) m i")
                n, d = (a[:].rearrange("p (m i r) -> p r m i", m=SEQ // P, r=16) for a in (num, den))
                r = slice(4 * m, 4 * m + 4)
                nc.gpsimd.tensor_tensor(y[:, r], n[:, r], d[:, r], ALU.mult).then_inc(y_done, 1)

            pool.sem_inc(y_done, 1)
            pool.sem_inc(den_ready, 2)
            pool.sem_inc(lo_done, 2)
            for n in range(2, 9):
                split_lo(n, n % 2)

            def pair(ch, j, splits):
                for u in range(2, UNITS):
                    f = u // 2 + 1
                    if u % 2 == 0 and 3 <= f <= splits:
                        split_lo(10 * j + (6 + f), f % 2)
                    if u % 2 == 0 and OT_BY_UNIT[u - 1][0] >= 4:
                        merge(ch, j, OT_BY_UNIT[u - 1][0])
                    if u == UNITS - 2:
                        merge(ch, j, OT_BY_UNIT[u - 1][1])
                gated(j, 8)
                merge(ch, j, 10)
                if splits == 10:
                    split_lo(10 * j + 17, 1)
                gated(j, 9)
                merge(ch, j, 11)

            POOL_STEPS = 4 + 4 * 4
            with pool.Fori(0, PAIRS - 1) as j:
                ch = Chain(pool, g_step, POOL_STEPS * j)
                pair(ch, j, 10)
                assert ch.n == POOL_STEPS, ch.n
                split_lo(10 * j + 18, 0)
                gated(j, 10)
                gated(j, 11)
            pair(Chain(pool, g_step, POOL_STEPS * (PAIRS - 1)), PAIRS - 1, 3)
            gated(PAIRS - 1, 10)
            gated(PAIRS - 1, 11)

        @block.tensor
        def _(pe):
            def project(unit, par, tile, slot, half, part):
                if part == 0:
                    pe.wait_ge(lo_done, tile + 1)
                    pe.wait_ge(pp_free, unit + 1)
                for k in (2 * part, 2 * part + 1):
                    for n, (w, h) in enumerate(((w_hi, "h_hi"), (w_hi, "h_lo"), (w_lo, "h_hi"))):
                        last = nc.tensor.matmul(
                            pp[:, par, :], w[:, slot, k, :],
                            keep[h][:, k, half * HALF:(half + 1) * HALF],
                            start=(k == 0 and n == 0), stop=(k == KT - 1 and n == 2))
                if part == 3:
                    last.then_inc(pp_full, 1)

            def scores(j, u):
                g, h, n0, nt, w = unit_of(u)
                if u == 0:
                    pe.wait_ge(pp_free, 20 * j + 8)
                if u == 8:
                    pe.wait_ge(pp_free, 20 * j + 14)
                if u == 16:
                    pe.wait_ge(pp_free, 20 * j + 20)
                pe.wait_ge(s_free, UNITS * j + (u + 1))
                rows = slice(HD * h, HD * h + HD)
                for t in range(nt):
                    n = n0 + t
                    k0 = (P * n, 256 * (n // 2), P * n)[g]
                    last = nc.tensor.matmul(sp_[:, u % 2, t * w:(t + 1) * w],
                                            qT[g][rows, P * n:P * n + P],
                                            kT[g][rows, k0:k0 + w], start=True, stop=True)
                last.then_inc(s_full, 1)

            def transpose_probs(j, u, at, par):
                pe.wait_ge(p_ready, UNITS * j + (u + 1))
                pe.wait_ge(t_free, T0 + at + 1)
                for c in range(4):
                    last = nc.tensor.transpose(tp[:, par, c * P:(c + 1) * P],
                                               prob[:, u % 2, c * P:(c + 1) * P], ident[:])
                last.then_inc(t_full, 1)

            def transpose_v(at, par, half, units_done):
                pe.wait_ge(pp_free, units_done)
                pe.wait_ge(t_free, at + 1)
                for c in range(4):
                    c0 = half * HALF + c * P
                    last = nc.tensor.transpose(tp[:, par, c * P:(c + 1) * P],
                                               vT[:, c0:c0 + P], ident[:])
                last.then_inc(t_full, 1)

            def values(j, u, at):
                g, h, n0, nt, w = unit_of(u)
                pe.wait_ge(t_free, T0 + at + 3)
                pe.wait_ge(o_free, UNITS * j + (u + 1))
                for t in range(nt):
                    n = n0 + t
                    keys = ((n, (n + 1) % 8), (n // 2 * 2, n // 2 * 2 + 1), (n,))[g]
                    for i, kt in enumerate(keys):
                        c = t * len(keys) + i
                        last = nc.tensor.matmul(op[:, u % 2, t * HD:(t + 1) * HD],
                                                probT[:, u % 2, c * P:(c + 1) * P],
                                                v[g][:, kt, HD * h:HD * h + HD],
                                                start=(i == 0), stop=(i == len(keys) - 1))
                last.then_inc(o_full, 1)

            def merge_transposes(j, u, e):
                t0 = 2 * (e - OT_BY_UNIT[u][0])
                pe.wait_ge(o_ready, UNITS * j + (u + 1))
                pe.wait_ge(ot_free, NE * j + (e + 1))
                for t in range(2):
                    nc.tensor.transpose(ot[:, t * P:(t + 1) * P], o_st[:, t0 + t, :], ident[:])
                    last = nc.tensor.transpose(ot[:, 256 + t * P:256 + (t + 1) * P],
                                               lse[:, t0 + t, :], ident[:])
                last.then_inc(ot_full, 1)

            for un in range(12):
                for part in range(4):
                    project(un, un % 2, un // 2, un // 2 % 2, un % 2, part)
                if un in (3, 9):
                    for half in range(2):
                        at = (0 if un == 3 else 2) + half
                        transpose_v(at, at % 2, half, (4 if un == 3 else 10))
            scores(0, 0)
            scores(0, 1)

            def pair(j, table, tiles, last_pair):
                base_u = 20 * j + 12
                base_t = NT * j

                def proj(u, part):
                    q = 4 * u + part
                    if last_pair and u >= 2:
                        if part % 2:
                            return
                        q = 8 + 2 * (u - 2) + part // 2
                    n = q // 4
                    if n < 2 * tiles:
                        project(base_u + n, n % 2, 10 * j + (6 + n // 2), (n // 2) % 2, n % 2, q % 4)

                def probs_t(u):
                    n = table[("p", u)]
                    transpose_probs(j, u, base_t + n, n % 2)

                for u in range(UNITS):
                    if 1 <= u < UNITS - 1:
                        scores(j, u + 1)
                    if u == UNITS - 1:
                        probs_t(u)
                    if u % 2 == 0 and u >= 2:
                        merge_transposes(j, u - 1, OT_BY_UNIT[u - 1][0])
                    proj(u, 0)
                    proj(u, 1)
                    if u < UNITS - 1:
                        probs_t(u)
                    else:
                        values(j, u, base_t + table[("p", u)])
                    if u == UNITS - 2:
                        merge_transposes(j, u - 1, OT_BY_UNIT[u - 1][1])
                    proj(u, 2)
                    if u == UNITS - 1:
                        merge_transposes(j, u, OT_BY_UNIT[u][0])
                    proj(u, 3)
                    if u < UNITS - 1:
                        values(j, u, base_t + table[("p", u)])
                    if u in V_AT and ("v", V_AT[u], 0) in table:
                        for half in range(2):
                            n = table[("v", V_AT[u], half)]
                            transpose_v(base_t + (T0 + n), n % 2, half, base_u + (u + 1))
                if not last_pair:
                    scores(j + 1, 0)
                merge_transposes(j, UNITS - 1, OT_BY_UNIT[UNITS - 1][1])
                if not last_pair:
                    scores(j + 1, 1)

            with pe.Fori(0, PAIRS - 1) as j:
                pair(j, T_AT, 10, False)
            pair(PAIRS - 1, T_LAST, 4, True)

        @block.scalar
        def _(act):
            def split_hi(n, slot, rounds):
                act.wait_ge(w_in[slot], rounds * 16)
                act.wait_ge(pp_full, 2 * (n - 2) + 2)
                nc.scalar.activation(w_hi[:, slot].rearrange("p k c -> p (k c)"),
                                     w_raw[:, slot].rearrange("p k c -> p (k c)"),
                                     ACT.Copy).then_inc(hi_done, 1)

            def put(dst, src, **kw):
                return nc.scalar.activation(dst, src, ACT.Copy, **kw)

            def evacuate(j, unit, par, kind, half, scale_col):
                act.wait_ge(pp_full, unit + 1)
                src = pp[:, par, :]
                t0 = half * HALF
                if kind == GATE:
                    if half == 0:
                        act.wait_ge(y_done, 4 * j + 1)
                    put(gate[:, t0:t0 + HALF], src).then_inc(pp_free, 1)
                    return
                g, which = TILE_GROUP[kind]
                buf = (qT[g], kT[g], vT)[which]
                kw = {"scale": qscale[:, scale_col:scale_col + 1]} if which == 0 else {}
                if g == 0 and which > 0:
                    if half == 0:
                        if which == 1:
                            put(buf[:, SEQ + RADIUS:KC0], src[:, 0:RADIUS])
                        ins = put(buf[:, RADIUS:RADIUS + HALF], src)
                    elif which == 1:
                        put(buf[:, 0:RADIUS], src[:, HALF - RADIUS:HALF])
                        ins = put(buf[:, RADIUS + HALF:RADIUS + SEQ], src)
                    else:
                        put(buf[:, 0:RADIUS], src[:, HALF - RADIUS:HALF])
                        ins = put(buf[:, RADIUS + HALF:SEQ], src[:, 0:HALF - RADIUS])
                elif g == 0:
                    ins = put(buf[:, t0:t0 + HALF], src, **kw)
                else:
                    d = DILS[g]
                    dst = buf[:, 0:SEQ].rearrange("p (r i) -> p i r", r=d)
                    ins = put(dst[:, t0 // d:(t0 + HALF) // d, :],
                              src.rearrange("p (i r) -> p i r", r=d), **kw)
                ins.then_inc(pp_free, 1)

            def softmax(j, u):
                g, h, n0, nt, w = unit_of(u)
                act.wait_ge(top_ready, UNITS * j + (u + 1))
                for t in range(nt):
                    last = nc.scalar.activation(prob[:, u % 2, t * w:(t + 1) * w],
                                                prob[:, u % 2, t * w:(t + 1) * w], ACT.Exp,
                                                bias=ntop[:, u % 4, t:t + 1],
                                                accum_out=z[:, u % 4, t:t + 1])
                last.then_inc(p_ready, 1)
                act.wait_ge(p_ready, UNITS * j + (u + 1))
                nc.scalar.activation(lnz[:, u % 4, 0:nt], z[:, u % 4, 0:nt],
                                     ACT.Ln).then_inc(lnz_ready, 1)

            def weights(j, u, e):
                if e >= 4:
                    act.wait_ge(diff_ready, 8 * j + (e - 3))
                    if e >= 8:
                        nc.scalar.activation(like(mx[:, e % 2, :], e), tokens(gate, e), ACT.Exp,
                                             scale=-1.0)
                    flat = ee[:, e % 2].rearrange("p a c -> p (a c)")
                    nc.scalar.activation(flat, flat, ACT.Exp).then_inc(wt_ready, 1)

            act.preload_act_table_set("natural_log_exp_and_others")
            act.sem_inc(pp_free, 2)
            act.sem_inc(hi_done, 2)
            act.wait_ge(const_in, 48)
            for un in range(12):
                if un >= 1:
                    if un - 1 == 6:
                        act.wait_ge(t_full, 2)
                    evacuate(0, un - 1, (un - 1) % 2, FIRST_TILES[(un - 1) // 2], (un - 1) % 2, 0)
                if un % 2 == 0 and un >= 2:
                    n = un // 2 + 1
                    act.wait_ge(w_in[n % 2], 16 * (n // 2 + 1))
                    act.wait_ge(pp_full, 2 * (n - 2) + 2)
                    nc.scalar.activation(w_hi[:, n % 2].rearrange("p k c -> p (k c)"),
                                         w_raw[:, n % 2].rearrange("p k c -> p (k c)"),
                                         ACT.Copy).then_inc(hi_done, 1)
            evacuate(0, 11, 1, K1, 1, 0)
            softmax(0, 0)

            def pair(j, table, kinds, last_pair):
                base_u = 20 * j + 12
                units = 2 * len(kinds)
                evac_at = {u: u - 1 for u in range(1, units + 1)}
                split_at = {u: u // 2 + 1 for u in range(0, UNITS, 2)}
                if last_pair:
                    evac_at = {1: 0, 2: 1, **{2 * n: n for n in range(2, units)}}
                    split_at = {0: 1, 2: 2, 6: 3}
                for u in range(UNITS):
                    if u in evac_at:
                        n = evac_at[u]
                        k = kinds[n // 2]
                        first_half = n % 2 == 0
                        if k in (VT2, VT0, VT1) and first_half:
                            before = {VT2: None, VT0: ("v", 2, 1), VT1: ("v", 0, 1)}[k]
                            act.wait_ge(t_full, T0 + NT * j + (table[before] + 1 if before else 0))
                        evacuate(j, base_u + n, n % 2, k, n % 2, 0 if k == Q2 else 1)
                    if u >= 1:
                        softmax(j, u)
                    if u in split_at:
                        f = split_at[u]
                        split_hi(10 * j + (6 + f), f % 2, 5 * j + (3 + f // 2 + 1))
                    if u % 2 == 0 and u >= 2:
                        weights(j, u - 1, OT_BY_UNIT[u - 1][0])
                    if u == UNITS - 2:
                        weights(j, u - 1, OT_BY_UNIT[u - 1][1])
                if not last_pair:
                    evacuate(j, base_u + 19, 1, kinds[9], 1, 1)
                    softmax(j + 1, 0)
                weights(j, UNITS - 1, OT_BY_UNIT[UNITS - 1][0])
                weights(j, UNITS - 1, OT_BY_UNIT[UNITS - 1][1])
                if not last_pair:
                    nc.scalar.activation(qscale[:], qscale[:], ACT.Copy,
                                         scale=2.0).then_inc(scale_set, 1)
                    act.wait_ge(scale_set, j + 1)

            with act.Fori(0, PAIRS - 1) as j:
                pair(j, T_AT, STEP_TILES, False)
            pair(PAIRS - 1, T_LAST, LAST_TILES, True)

        @block.vector
        def _(dve):
            def tops(ch, j, u):
                g, h, n0, nt, w = unit_of(u)
                dve.wait_ge(s_full, UNITS * j + (u + 1))
                dve.sem_inc(tops_begun, 1)
                for t in range(nt):
                    c0, cw = bias_columns(g, n0 + t)
                    last = nc.vector.tensor_tensor_reduce(
                        out=prob[:, u % 2, t * w:(t + 1) * w], in0=sp_[:, u % 2, t * w:(t + 1) * w],
                        in1=bias[:, c0:c0 + cw], scale=slope[:, h:h + 1], scalar=-3e38,
                        op0=ALU.add, op1=ALU.max, accum_out=top[:, u % 4, t:t + 1])
                last.then_inc(s_free, 1)
                dve.wait_ge(s_free, UNITS * j + (u + 3))
                nc.vector.tensor_scalar(ntop[:, u % 4, 0:nt], top[:, u % 4, 0:nt], -1.0, None,
                                        ALU.mult).then_inc(top_ready, 1)

            def copy_t(ev, at, par, j, u):
                dve.wait_ge(t_full, at + 1)
                if ev[0] == "p":
                    dst = probT[:, u % 2, :]
                else:
                    dst = v[ev[1]][:, 4 * ev[2]:4 * ev[2] + 4, :].rearrange("p a c -> p (a c)")
                nc.vector.tensor_copy(dst, tp[:, par, :]).then_inc(t_free, 1)

            def outputs(ch, j, u):
                g, h, n0, nt, w = unit_of(u)
                dve.wait_ge(lnz_ready, UNITS * j + (u + 1))
                ch.link(nc.vector.reciprocal(rz[:, u % 4, 0:nt], z[:, u % 4, 0:nt]))
                dve.wait_ge(o_full, UNITS * j + (u + 1))
                nc.vector.tensor_tensor(o_st[:, 0:nt, HD * h:HD * h + HD],
                                        op[:, u % 2, 0:nt * HD].rearrange("p (t c) -> p t c", t=nt),
                                        bcast(rz[:, u % 4, 0:nt], HD), ALU.mult).then_inc(o_free, 1)
                nc.vector.tensor_tensor(lse[:, 0:nt, HD * h:HD * h + HD],
                                        bcast(top[:, u % 4, 0:nt], HD),
                                        bcast(lnz[:, u % 4, 0:nt], HD), ALU.add).then_inc(o_ready, 1)

            def merge_in(ch, j, e):
                dve.wait_ge(ot_full, NE * j + (e + 1))
                if e < 4:
                    if e == 0:
                        dve.wait_ge(y_done, 4 * j + 1)
                    nc.vector.tensor_copy(tokens(num, e), ot[:, 0:256])
                    nc.vector.tensor_copy(tokens(ref, e), ot[:, 256:512]).then_inc(ot_free, 1)
                    return
                st = stage[:, e % 2]
                if 6 <= e < 10:
                    dve.wait_ge(stage_used, 4 * j + (e - 5))
                else:
                    dve.wait_ge(den_ready, 4 * j + ((e - 5) if e < 6 else (e - 9)) + 2)
                nc.vector.tensor_copy(st.rearrange("p a c -> p (a c)"), ot[:, :]).then_inc(ot_free, 1)
                dve.wait_ge(ot_free, NE * j + (e + 2))
                lb = like(st[:, 1, :], e)
                m = like(mx[:, e % 2, :], e)
                ch.link(nc.vector.tensor_tensor(m, tokens(ref, e), lb, ALU.max))
                ch.link(nc.vector.tensor_tensor(like(ee[:, e % 2, 0, :], e), tokens(ref, e), m,
                                                ALU.subtract))
                nc.vector.tensor_tensor(like(ee[:, e % 2, 1, :], e), lb, m,
                                        ALU.subtract).then_inc(diff_ready, 1)
                if e < 8:
                    ch.link(nc.vector.tensor_copy(tokens(ref, e), m))

            def invert(j, e):
                dve.wait_ge(den_ready, 4 * j + (e - 7) + 2)
                dv = tokens(den, e)
                nc.vector.reciprocal(dv, dv).then_inc(den_inverse, 1)

            dve.sem_inc(s_free, 2)
            dve.sem_inc(t_free, 2)
            dve.sem_inc(o_free, 2)
            dve.sem_inc(ot_free, 1)
            dve.wait_ge(const_in, 48)
            for at in range(T0):
                copy_t(("v", at // 2, at % 2), at, at % 2, 0, 0)
            ch0 = Chain(dve, v_step, 0)
            tops(ch0, 0, 0)
            tops(ch0, 0, 1)
            assert ch0.n == 0

            def step(ch, j, u, table):
                if 1 <= u < UNITS - 1:
                    tops(ch, j, u + 1)
                if u % 2 == 0 and u >= 2:
                    merge_in(ch, j, OT_BY_UNIT[u - 1][0])
                ev = ("p", u)
                copy_t(ev, T0 + NT * j + table[ev], table[ev] % 2, j, u)
                if u == UNITS - 2:
                    merge_in(ch, j, OT_BY_UNIT[u - 1][1])
                outputs(ch, j, u)
                if u in V_AT and ("v", V_AT[u], 0) in table:
                    for half in range(2):
                        ev = ("v", V_AT[u], half)
                        copy_t(ev, T0 + NT * j + table[ev], table[ev] % 2, j, u)

            def pair(ch, j, table, last_pair):
                for u in range(2, UNITS):
                    step(ch, j, u, table)
                invert(j, 8)
                if not last_pair:
                    ch.link(nc.vector.tensor_scalar(slope[:], slope[:], 0.5, None, ALU.mult))
                    tops(ch, j + 1, 0)
                a, b = OT_BY_UNIT[UNITS - 1]
                merge_in(ch, j, a)
                merge_in(ch, j, b)
                if not last_pair:
                    tops(ch, j + 1, 1)
                invert(j, 9)
                if not last_pair:
                    step(ch, j + 1, 0, table)
                invert(j, a)
                if not last_pair:
                    step(ch, j + 1, 1, table)
                invert(j, b)

            STEPS = 41
            for u in range(2):
                step(ch0, 0, u, T_AT)
            with dve.Fori(0, PAIRS - 1) as j:
                ch = Chain(dve, v_step, ch0.n + STEPS * j)
                pair(ch, j, T_AT, False)
                assert ch.n == STEPS, ch.n
            pair(Chain(dve, v_step, ch0.n + STEPS * (PAIRS - 1)), PAIRS - 1, T_LAST, True)

def output_phase(nc, io, keep, layer):
    is_b = layer == 1
    CPM = 2 if is_b else 1
    KO = KT * CPM
    MT = SEQ // P
    BODY = 4
    TURNS = CPM * MT // BODY
    MPB = BODY // CPM
    with ExitStack() as ctx:
        def sb(name, shape, dt=F32):
            return ctx.enter_context(nc.sbuf_tensor(f"{name}_o{layer}", shape, dt))

        def sem(name):
            return ctx.enter_context(nc.semaphore(f"{name}_o{layer}"))

        ADA = 0 if is_b else KT
        ARING = 2
        trunk = keep["trunk"][:].rearrange("p (m d) -> p m d", m=MT)
        w_raw = trunk[:, 5:8] if is_b else sb("w_raw", [P, 3, D])
        w_hi = sb("w_hi", [P, KO, D], F32R)
        w_lo = sb("w_lo", [P, KO, D], F32R)
        y_hi = sb("y_hi", [P, 2, KT, P], F32R)
        y_lo = sb("y_lo", [P, 2, KT, P], F32R)
        rows = sb("rows", [P, 3, D])
        x_in = sb("x_in", [P, 2, D])
        x_new = trunk[:, 0:2] if is_b else trunk
        stats = sb("stats", [P, 2, 6])
        mv = sb("mv", [P, 2])
        sd = sb("sd", [P, 3])
        if is_b:
            y_raw = keep["trunk"][:, 2 * D:4 * D].rearrange("p (b k c) -> p b k c", b=2, k=KT)
            sq = trunk[:, 4].rearrange("p (k c) -> p k c", k=KT)
            sqs = sb("sqs", [P, 2, P])
            nw = sb("nw", [P, KO])
            ones = sb("ones", [P, 1])
            rms = sb("rms", [P, 3])
            ps_q = ctx.enter_context(nc.psum_tensor("ps_q", [P, 2, HALF], F32))
        else:
            ada_ring = sb("ada_ring", [P, ARING, 3 * D])
            ada_acc = sb("ada_acc", [P, 3 * D])
            brow = sb("ada_b_row", [1, D])
            bcol = sb("ada_b_cols", [P, 2 * KT])
            ones = sb("ones", [P, P])
            gate_sb = sb("gate_sb", [1, D])
            ps_col = ctx.enter_context(nc.psum_tensor("ps_col1", [P, HALF], F32))
            ps_gate = ctx.enter_context(nc.psum_tensor("ps_gate1", [P, 2, HALF], F32))
            ada_in = [sem(f"ada_in{i}") for i in range(ARING)]
            b_in, ada_used = sem("b_in"), sem("ada_used")
            col_full, gate_full = sem("col_full"), sem("gate_full")
            gate_copied, gate_out = sem("gate_copied"), sem("gate_out")
            mods = keep["mods"]
        acc = ctx.enter_context(nc.psum_tensor(f"acc_o{layer}", [P, 2, 2, HALF], F32))

        w_in = [sem(f"w_in{i}") for i in range(3)]
        w_hi_done, w_lo_done = sem("w_hi_done"), [sem("w_lo_done0"), sem("w_lo_done1")]
        rows_in, ones_set = sem("rows_in"), sem("ones_set")
        y_in = [sem("y_in0"), sem("y_in1")]
        x_arr = [sem("x_arr0"), sem("x_arr1")]
        nw_in, y_hi_done, y_lo_done = sem("nw_in"), sem("y_hi_done"), sem("y_lo_done")
        chunk_done, acc_free = sem("chunk_done"), sem("acc_free")
        t_added, var_ready, root_done = sem("t_added"), sem("var_ready"), sem("root_done")
        normed, scaled, out_ready = sem("normed"), sem("scaled"), sem("out_ready")
        out_sent = [sem("out_sent0"), sem("out_sent1")]
        sq_full, sq_sum, ms_ready, rms_root = sem("sq_full"), sem("sq_sum"), sem("ms_ready"), sem("rms_root")
        stats_whole = sem("stats_whole")
        v_step = sem("v_step")

        block = ctx.enter_context(nc.Block())

        def in_turns(eng, turn):
            if TURNS > 2:
                with eng.Fori(0, TURNS - 1) as it:
                    turn(it, False)
            else:
                turn(0, False)
            turn(TURNS - 1, True)

        def x_new_tile(it, s):
            return x_new[:, s % 2, :] if is_b else x_new[:, MPB * it + s, :]

        def it_is_first(it):
            return isinstance(it, int) and it == 0

        def y_tile(g):
            return keep["trunk"][:].rearrange("p (m k t) -> p m k t", m=MT, k=KT)[:, g]

        @block.sync
        def _(sp):
            def load_w(k):
                if k >= 3:
                    sp.wait_ge(w_lo_done[(k - 3) % 2], (k - 3) // 2 + 1)
                sp.dma_start(w_raw[:, k % 3, :], io["w_out"][P * k:P * k + P, :]
                             ).then_inc(w_in[k % 3], 16)

            def load_y(m, c):
                k0 = KT * (c % CPM)
                src = io["yT"][m]
                sp.dma_start(y_raw[:, c % 2], src[:, k0:k0 + KT, :]).then_inc(y_in[c % 2], 16)

            if is_b:
                sp.dma_start(nw[:], io["norm_w"]).then_inc(nw_in, 16)
                load_y(0, 0)
            for k in range(KO):
                load_w(k)
                if is_b and k == 3:
                    load_y(0, 1)
                if k == 5:
                    for m in range(2):
                        sp.dma_start(x_in[:, m, :], io["x_rows"][m]).then_inc(x_arr[m], 16)
            for k in range(min(ADA, ARING)):
                sp.dma_start(ada_ring[:, k, :], io["ada_w"][1, P * k:P * k + P, :]
                             ).then_inc(ada_in[k], 16)
            if ADA:
                sp.dma_start(brow[:], io["ada_b"][:, 1, 2 * D:3 * D]).then_inc(b_in, 16)
                sp.dma_start(bcol[:], io["ada_b_cols"][1]).then_inc(b_in, 16)

            def next_x(it, s):
                sp.wait_ge(t_added, MPB * it + (s + 1))
                sp.dma_start(x_in[:, s % 2, :], io["x_rows"][MPB * it + (s + 2)]
                             ).then_inc(x_arr[s % 2], 16)

            def store(it, s):
                sp.wait_ge(out_ready, MPB * it + (s + 1))
                sp.dma_start(io["x_out"][MPB * it + s], x_new_tile(it, s)
                             ).then_inc(out_sent[s % 2], 16)

            def turn(it, last):
                for c in range(BODY):
                    if is_b and not (last and c >= 2):
                        sp.wait_ge(sq_sum, BODY * it + (c + 1))
                        sp.wait_ge(y_lo_done, BODY * it + (c + 1))
                        load_y(MPB * it + (c + 2) // 2, c)
                    s = c // CPM
                    if c % CPM == CPM - 1 and not (last and s >= MPB - 2):
                        next_x(it, s)
                    if not is_b:
                        for k in range(2 * s + ARING, 2 * s + ARING + 2):
                            if it_is_first(it) and k < ADA:
                                sp.wait_ge(ada_used, k - ARING + 1)
                                sp.dma_start(ada_ring[:, k % ARING, :],
                                             io["ada_w"][1, P * k:P * k + P, :]
                                             ).then_inc(ada_in[k % ARING], 16)
                        store(it, s)
                if is_b:
                    for s in range(MPB):
                        store(it, s)
            in_turns(sp, turn)
            if ADA:
                sp.wait_ge(gate_copied, 1)
                sp.dma_start(io["gate_row"][1:2, :], gate_sb[:]).then_inc(gate_out, 16)
                sp.wait_ge(gate_out, 16)
            for s in range(2):
                sp.wait_ge(out_sent[s], 16 * (MT // 2 + 1))

        @block.gpsimd
        def _(pool):
            pool.memset(ones[:], 1.0).then_inc(ones_set, 1)
            for k in range(0, 0 if is_b else KO, 2):
                pool.wait_ge(w_hi_done, k + 1)
                nc.gpsimd.tensor_tensor(w_lo[:, k, :], w_raw[:, k % 3, :], w_hi[:, k, :].bitcast(F32),
                                        ALU.subtract).then_inc(w_lo_done[0], 1)

            def squares(it, c):
                g = BODY * it + c
                pool.wait_ge(y_in[c % 2], 16 * (2 * it + c // 2 + 1))
                if not (isinstance(it, int) and g == 0):
                    pool.wait_ge(sq_sum, g)
                if not (isinstance(it, int) and g < 2):
                    pool.wait_ge(chunk_done, g - 1)
                nc.gpsimd.tensor_tensor(sq, y_raw[:, c % 2], y_raw[:, c % 2],
                                        ALU.mult).then_inc(sq_full, 1)
                pool.wait_ge(sq_full, 4 * g + 1)
                for n, half in enumerate((4, 2, 1)):
                    out = sqs[:, c % 2:c % 2 + 1, :] if half == 1 else sq[:, 0:half]
                    nc.gpsimd.tensor_tensor(out, sq[:, 0:half], sq[:, half:2 * half],
                                            ALU.add).then_inc(sq_full if half > 1 else sq_sum, 1)
                    if half > 1:
                        pool.wait_ge(sq_full, 4 * g + 2 + n)
                pool.sem_inc(sq_full, 1)

            if is_b:
                squares(0, 0)
                squares(0, 1)
            pool.wait_ge(rows_in, 16 * 3)

            def turn(it, last):
                for s in range(MPB):
                    if is_b:
                        for c in (2 * s, 2 * s + 1):
                            if not last and c < 2:
                                squares(it, c + 2)
                            elif not last:
                                squares(it + 1, c - 2)
                            elif c < 2:
                                squares(it, c + 2)
                    if last and s == MPB - 1:
                        continue
                    pool.wait_ge(normed, MPB * it + (s + 1))
                    nc.gpsimd.tensor_tensor(x_new_tile(it, s), x_new_tile(it, s), rows[:, 1, :],
                                            ALU.mult).then_inc(scaled, 1)
                    pool.wait_ge(scaled, MPB * it + (s + 1))
                    nc.gpsimd.tensor_tensor(x_new_tile(it, s), x_new_tile(it, s), rows[:, 2, :],
                                            ALU.add).then_inc(out_ready, 1)
            in_turns(pool, turn)

        @block.scalar
        def _(act):
            def load_rows():
                for n, src in enumerate((io["gate_row"], io["ln_g"], io["ln_b"])):
                    act.dma_start(rows[:, n, :], src[layer].partition_broadcast(P)
                                  ).then_inc(rows_in, 16)

            def split_y(it, c):
                g = BODY * it + c
                if is_b:
                    act.wait_ge(y_in[c % 2], 16 * (2 * it + c // 2 + 1))
                    src = y_raw[:, c % 2]
                else:
                    src = y_tile(g)
                nc.scalar.activation(y_hi[:, c % 2], src, ACT.Copy).then_inc(y_hi_done, 1)

            if is_b:
                act.wait_ge(nw_in, 16)
            split_y(0, 0)
            for k in range(KO):
                act.wait_ge(w_in[k % 3], 16 * (k // 3 + 1))
                nc.scalar.activation(w_hi[:, k, :], w_raw[:, k % 3, :], ACT.Copy,
                                     scale=nw[:, k:k + 1] if is_b else 1.0).then_inc(w_hi_done, 1)
                if k == 5:
                    load_rows()
                if k == 6:
                    split_y(0, 1)

            def turn(it, last):
                for c in range(BODY):
                    if not (last and c >= 2):
                        act.wait_ge(chunk_done, BODY * it + (c + 1))
                        if c < 2:
                            split_y(it, c + 2)
                        else:
                            split_y(it + 1, c - 2)
                    if c % CPM == CPM - 1:
                        m = MPB * it + c // CPM
                        if is_b:
                            act.wait_ge(ms_ready, m + 1)
                            nc.scalar.activation(rms[:, 1:2], rms[:, 0:1], ACT.Sqrt).then_inc(rms_root, 1)
                        act.wait_ge(var_ready, m + 1)
                        nc.scalar.activation(sd[:, 1:2], sd[:, 0:1], ACT.Sqrt).then_inc(root_done, 1)
            in_turns(act, turn)

        @block.vector
        def _(dve):
            def y_rest(it, c):
                dve.wait_ge(y_hi_done, BODY * it + (c + 1))
                nc.vector.tensor_tensor(y_lo[:, c % 2], y_raw[:, c % 2] if is_b else
                                        y_tile(BODY * it + c), y_hi[:, c % 2].bitcast(F32),
                                        ALU.subtract).then_inc(y_lo_done, 1)

            def w_rest(k):
                dve.wait_ge(w_hi_done, k + 1)
                hi = w_hi[:, k, :].bitcast(F32)
                if is_b:
                    ins = nc.vector.scalar_tensor_tensor(w_lo[:, k, :], w_raw[:, k % 3, :],
                                                         nw[:, k:k + 1], hi, ALU.mult, ALU.subtract)
                else:
                    ins = nc.vector.tensor_tensor(w_lo[:, k, :], w_raw[:, k % 3, :], hi, ALU.subtract)
                ins.then_inc(w_lo_done[k % 2], 1)

            def normalise(ch, it, s):
                m = MPB * it + s
                b = s % 2
                dve.wait_ge(chunk_done, CPM * m + CPM)
                if is_b:
                    ch.link(nc.vector.tensor_scalar(rms[:, 0:1], ps_q[:, b, 0:1], 1.0 / (2 * D),
                                                    RMS_EPS, ALU.mult, ALU.add))
                    dve.sem_inc(ms_ready, 1)
                    dve.wait_ge(rms_root, m + 1)
                    ch.link(nc.vector.reciprocal(rms[:, 2:3], rms[:, 1:2]))
                scale = rms[:, 2:3] if is_b else 1.0
                t = x_new_tile(it, s)
                if is_b:
                    dve.wait_ge(out_sent[b], 16 * (MPB // 2 * it + (s // 2 + 1)))
                for n in range(2):
                    ins = nc.vector.scalar_tensor_tensor(
                        t[:, n * HALF:(n + 1) * HALF], acc[:, b, n, :], scale,
                        rows[:, 0, n * HALF:(n + 1) * HALF], ALU.mult, ALU.mult)
                ins.then_inc(acc_free, 1)
                dve.wait_ge(x_arr[b], 16 * (MPB // 2 * it + (s // 2 + 1)))
                dve.wait_ge(acc_free, m + 3)
                nc.vector.scalar_tensor_tensor(t, x_in[:, b, :], ALPHA, t, ALU.mult,
                                               ALU.add).then_inc(t_added, 1)
                dve.wait_ge(t_added, m + 1)
                nc.vector.bn_stats(stats[:, 0, :], t[:, 0:HALF])
                ch.link(nc.vector.bn_stats(stats[:, 1, :], t[:, HALF:D]))
                dve.sem_inc(stats_whole, 1)
                ch.link(nc.vector.bn_aggr(mv[:], stats[:].rearrange("p a b -> p (a b)")))
                nc.vector.tensor_scalar(sd[:, 0:1], mv[:, 1:2], LN_EPS, None,
                                        ALU.add).then_inc(var_ready, 1)
                dve.wait_ge(root_done, m + 1)
                ch.link(nc.vector.reciprocal(sd[:, 2:3], sd[:, 1:2]))
                nc.vector.tensor_scalar(t, t, mv[:, 0:1], sd[:, 2:3], ALU.subtract,
                                        ALU.mult).then_inc(normed, 1)
                if isinstance(it, int) and m == MT - 1:
                    dve.wait_ge(normed, MT)
                    ch.link(nc.vector.tensor_tensor(t, t, rows[:, 1, :], ALU.mult))
                    dve.wait_ge(out_ready, MT - 1)
                    nc.vector.tensor_tensor(t, t, rows[:, 2, :], ALU.add).then_inc(out_ready, 1)

            dve.sem_inc(out_sent[0], 16)
            dve.sem_inc(out_sent[1], 16)
            def modulate(k):
                dve.wait_ge(ada_in[k % ARING], 16 * (k // ARING + 1))
                w, cond = ada_ring[:, k % ARING, :], keep["cond"][:, k:k + 1]
                if k == 0:
                    ins = nc.vector.tensor_scalar(ada_acc[:], w, cond, None, ALU.mult)
                else:
                    dve.wait_ge(ada_used, k)
                    ins = nc.vector.scalar_tensor_tensor(ada_acc[:], w, cond, ada_acc[:], ALU.mult,
                                                         ALU.add)
                ins.then_inc(ada_used, 1)

            def finish_modulation(ch):
                dve.wait_ge(col_full, 1)
                dve.wait_ge(b_in, 32)
                ch.link(nc.vector.tensor_tensor(mods[:, 1, :], ps_col[:, 0:2 * KT], bcol[:],
                                                ALU.add))
                nc.vector.tensor_scalar(mods[:, 1, KT:2 * KT], mods[:, 1, KT:2 * KT], 1.0, None,
                                        ALU.add)
                dve.wait_ge(gate_full, 1)
                nc.vector.tensor_copy(gate_sb[:], ps_gate[0:1, :, :].rearrange("p a b -> p (a b)")
                                      ).then_inc(gate_copied, 1)

            dve.sem_inc(acc_free, 2)
            ch0 = Chain(dve, v_step, 0)
            y_rest(0, 0)
            for k in range(KO):
                if is_b or k % 2 == 1:
                    w_rest(k)
                if k == 7:
                    y_rest(0, 1)
            dve.wait_ge(rows_in, 16 * 3)
            steps0 = ch0.n
            steps = 2 * 5 if is_b else 4 * 3

            def turn(it, last):
                ch = Chain(dve, v_step, steps0 + steps * it)
                for c in range(BODY):
                    if not (last and c >= 2):
                        if c < 2:
                            y_rest(it, c + 2)
                        else:
                            y_rest(it + 1, c - 2)
                    if c % CPM == CPM - 1:
                        normalise(ch, it, c // CPM)
                        if it_is_first(it):
                            for k in range(2 * (c // CPM), min(2 * (c // CPM) + 2, ADA)):
                                modulate(k)
                        elif not is_b and c == 3:
                            finish_modulation(ch)
                if not last:
                    assert ch.n == steps, ch.n
            in_turns(dve, turn)

        @block.tensor
        def _(pe):
            pe.wait_ge(ones_set, 1)

            def turn(it, last, first=False):
                for c in range(BODY):
                    g = BODY * it + c
                    s, b = c // CPM, c // CPM % 2
                    pe.wait_ge(y_lo_done, g + 1)
                    if c % CPM == 0:
                        pe.wait_ge(acc_free, MPB * it + (s + 1))
                    for k in range(KT):
                        kk = KT * (c % CPM) + k
                        if first and c < CPM:
                            pe.wait_ge(w_lo_done[kk % 2], kk // 2 + 1)
                        for n, (y, w) in enumerate(((y_hi, w_hi), (y_hi, w_lo), (y_lo, w_hi))):
                            for half in range(2):
                                last_mm = nc.tensor.matmul(
                                    acc[:, b, half, :], y[:, c % 2, k, :],
                                    w[:, kk, half * HALF:(half + 1) * HALF],
                                    start=(kk == 0 and n == 0), stop=(kk == KO - 1 and n == 2))
                    if is_b:
                        pe.wait_ge(sq_sum, g + 1)
                        last_mm = nc.tensor.matmul(ps_q[:, b, 0:1], sqs[:, c % 2, :], ones[:],
                                                   start=(c % CPM == 0), stop=(c % CPM == 1))
                    last_mm.then_inc(chunk_done, 1)
                    if not is_b and not it_is_first(it) and c == 2:
                        pe.wait_ge(b_in, 32)
                        pe.wait_ge(ada_used, KT)
                        modulation_products(nc, ada_acc, brow, ones, ps_col, ps_gate, col_full,
                                            gate_full)
            turn(0, False, True)
            if TURNS > 2:
                with pe.Fori(1, TURNS - 1) as it:
                    turn(it, False)
            turn(TURNS - 1, True)

SSM_INNER = 2 * D
SH = SSM_INNER // HD
NS = 128
GROUPS = 4
GH = SH // GROUPS
TAPS = 5
CH = SEQ // P
XB = 6
SSM_STEPS = 2 * CH

def stream_b():
    def xbc(g):
        c0 = SSM_INNER
        return ([c0 + (4 * g + i) * P for i in range(4)] + [c0 + SSM_INNER + g * NS]
                + [c0 + SSM_INNER + (GROUPS + g) * NS])
    order = xbc(0)
    for g in range(GROUPS):
        if g < GROUPS - 1:
            order += xbc(g + 1)
        order += [(4 * g + i) * P for i in range(4)]
    return order

def conv_channels():
    return [c - SSM_INNER for g in range(GROUPS) for c in
            ([SSM_INNER + (4 * g + i) * P for i in range(4)]
             + [2 * SSM_INNER + g * NS, 2 * SSM_INNER + (GROUPS + g) * NS])]

def state_space_phase(nc, io, keep):
    with ExitStack() as ctx:
        def sb(name, shape, dt=F32):
            return ctx.enter_context(nc.sbuf_tensor(name, shape, dt))

        def ps(name, shape):
            return ctx.enter_context(nc.psum_tensor(name, shape, F32))

        def sem(name):
            return ctx.enter_context(nc.semaphore(f"{name}_s"))

        GW = GH * HD
        w_raw = sb("w_raw_s", [P, KT, P])
        w_hi = sb("w_hi_s", [P, 2, KT, P], F32R)
        w_lo = sb("w_lo_s", [P, 2, KT, P], F32R)
        stage = sb("stage_s", [P, XB, SEQ])
        pad = sb("pad", [P, SEQ + TAPS - 1])
        th = sb("th", [P, 2, HALF])
        zs = sb("zs", [P, 2, HALF])
        trunk = keep["trunk"]
        x1 = trunk[:].rearrange("p (m d) -> p m d", m=CH)
        x = trunk[:, 0:CH * GW].rearrange("p (c w) -> p c w", c=CH)
        cT = sb("cT", [P, SEQ])
        bc = sb("bc", [P, CH, 2, P])
        y = trunk[:, CH * GW:2 * CH * GW].rearrange("p (c w) -> p c w", c=CH)
        em = sb("em", [P, 2, GH, P])
        xd = sb("xd", [P, 2, GW])
        xw = sb("xw", [P, GW])
        hs = sb("hs", [P, 2, GW])
        hd = sb("hd", [P, GW])
        yt = sb("yt", [P, GW])
        mask_raw = yt[:, 0:2 * P].rearrange("p (a b) -> p a b", a=2)
        yst = sb("yst", [P, 2, HALF])
        crow = sb("crow", [4 * GH, SEQ], F32R)
        sel_raw = sb("sel_raw", [4 * GH, 2 * GH])
        sel = sb("sel", [4 * GH, 2 * GH], F32R)
        mask = sb("mask", [P, 2, P], F32R)
        ident_r = sb("ident_r", [P, P], F32R)
        ident = keep["ident"]
        dskip = sb("dskip", [P, SH])
        conv = sb("conv", [P, GROUPS, XB * (TAPS + 1)])
        gneg, gout, gin, gtot, gdt = (sb(f"g{n}", [P, CH, 2, GH]) for n in
                                      ("neg", "out", "in", "tot", "dt"))
        gd = sb("gd", [P, GH])
        gconv = sb("gconv", [P, XB * (TAPS + 1)])

        pp = ps("pp_s", [P, 2, HALF])
        rows = ps("rows_s", [P, GH, P])
        bc_p = ps("bc_p", [P, 2, P])
        st_p = ps("st_p", [P, GW])
        yo_p = ps("yo_p", [P, GW])
        yd_p = ps("yd_p", [P, GW])
        W2 = 2 * SH
        h_tmp = em[:, 0].rearrange("p (b h) l -> p b (h l)", b=2)
        row_hi, row_lo = em[0:W2, 1].rearrange("p h l -> p (h l)"), cT[0:W2, :]

        def by_chunk(ap):
            return ap.rearrange("p (c w) -> p c w", c=CH)
        v, e, r, m = (by_chunk(b) for b in (xd[:, 0, :], xd[:, 1, :], hs[:, 0, :], hs[:, 1, :]))
        lg, ac, wd = by_chunk(hd[:]), by_chunk(xw[:]), by_chunk(yst[:, 0, :])
        tri = yst[:, 1, 0:3 * P].rearrange("p (a b) -> p a b", a=3)
        brow, arow = yt[:, 2 * P:2 * P + W2], yt[:, 2 * P + W2:2 * P + 2 * W2]
        bc_p2 = yo_p[:, 0:2 * P].rearrange("p (a b) -> p a b", a=2)
        dp, cum_p, tot_p = by_chunk(st_p[:]), yo_p, yd_p
        th_z = em[:, 0].rearrange("p (b h) l -> p b (h l)", b=2)
        fill = rows[:].rearrange("p (b h) l -> p b (h l)", b=2)

        names = ("hi_done lo_done pp_full pp_free conv_done tanh_done "
                 "silu_done loc_done sel_done rows_full exp_done "
                 "m_ready xd_ready xw_ready y_set st_full h_ready hd_ready yd_full "
                 "y_done yf_full y_gated xu_full xu_free c_moved pad_set gconv_done z_done v_step").split()
        S = {n: sem(n) for n in names}
        CONSTS = 16 * 8
        START = 2
        const_in, w_in, crow_in = sem("const_in"), sem("w_in"), sem("crow_in")
        y_out = [sem("y_out0"), sem("y_out1")]
        t_full, h_made, h_hi, h_lo = sem("t_full"), sem("h_made"), sem("h_hi"), sem("h_lo")
        dt_full, neg_abs, exped, logged = sem("dt_full"), sem("neg_abs"), sem("exped"), sem("logged")
        a_done, ac_ready, cum_full, cum_ready = (sem("a_done"), sem("ac_ready"), sem("cum_full"),
                                                 sem("cum_ready"))
        row_full, row_hi_done, row_lo_done, row_out = (sem("row_full"), sem("row_hi_done"),
                                                       sem("row_lo_done"), sem("row_out"))
        first_x_full, first_x_moved = sem("first_x_full"), sem("first_x_moved")
        sums_done, d_step = sem("sums_done"), sem("d_step")
        block = ctx.enter_context(nc.Block())

        def flat(ap):
            return ap.rearrange("p k c -> p (k c)")

        def wait(eng, name, count):
            eng.wait_ge(S[name], count + START)

        QPS = 3
        UB = 2 * XB

        def unit_step(u):
            return (4 * u + 3) // QPS

        CONV_STEP = {unit_step(2 * f + 1) + 1: f for f in range(XB)}
        EVAC_STEP = {}
        for u in range(UB):
            EVAC_STEP.setdefault(unit_step(u) + 1, []).append(u)
        SPLIT_AT = {0: 1}
        SPLIT_AT.update({unit_step(2 * f - 3) + 1: f for f in range(2, XB + 1)})
        SPLIT_AT.update({SSM_STEPS: XB + 1, 102: XB + 2, 104: XB + 3, 106: XB + 4})
        SPLIT_LAST = {0: 1, 4: 2, 8: 3}
        Z_STEP = {2 * u + 2: u for u in range(8)}

        def z_of(u):
            return stage[:, u // 2, u % 2 * HALF:(u % 2 + 1) * HALF]

        NU = 14

        def where(s):
            d = s // CH
            return d, (s if d == 0 else 2 * CH - 1 - s)

        def updates(s):
            return 7 * (s // CH) + s % CH

        @block.sync
        def _(sp):
            def load_w(n):
                wait(sp, "lo_done", n)
                sp.dma_start(flat(w_raw[:]), io["b_w"][n]).then_inc(w_in, 16)

            def load_rows(j):
                src = io["cum_rows"].rearrange("a (d h) t -> a d h t", d=2)
                for a in range(2):
                    for d in range(2):
                        r0 = (2 * a + d) * GH
                        sp.dma_start(crow[r0:r0 + GH, :].bitcast(F32),
                                     src[a, d, bass.ds(j * GH, GH), :]).then_inc(crow_in, 16)

            sp.dma_start(flat(w_raw[:]), io["b_w"][0]).then_inc(w_in, 16)
            for dst, src in ((wd, io["w_dt"]), (tri, io["tri"]),
                             (brow, io["dt_bias"][0].partition_broadcast(P)),
                             (arow, io["a_log"][0].partition_broadcast(P)), (mask_raw, io["mask"]), (sel_raw[:], io["sel"]),
                             (dskip[:], io["d_skip"][0].partition_broadcast(P)),
                             (conv[:], io["conv"])):
                sp.dma_start(dst, src).then_inc(const_in, 16)
            for n in range(1, 5):
                load_w(n)
            sp.wait_ge(row_hi_done, 2)
            sp.dma_start(io["cum_rows"][0], row_hi).then_inc(row_out, 16)
            sp.wait_ge(row_lo_done, 2)
            sp.dma_start(io["cum_rows"][1], row_lo).then_inc(row_out, 16)
            sp.wait_ge(row_out, 32)
            load_rows(0)
            for n in range(5, XB + 1):
                load_w(n)

            def group(j, last):
                for f in range(1, 4 if last else 10):
                    load_w(10 * j + (XB + f))
                    if f == 7:
                        wait(sp, "rows_full", SSM_STEPS * j + SSM_STEPS)
                        load_rows(j + 1)
                for i in range(8):
                    if i == 5 and not last:
                        load_w(10 * j + (XB + 10))
                    kt, hf = i // 2, i % 2
                    wait(sp, "y_gated", 8 * j + (i + 1))
                    dst = io["yT"][4 * hf:4 * hf + 4, :, bass.ds(4 * j + kt, 1), :]
                    sp.dma_start(dst.rearrange("m p a t -> p m (a t)"),
                                 yst[:, i % 2, :].rearrange("p (m t) -> p m t", m=4)
                                 ).then_inc(y_out[i % 2], 16)

            with sp.Fori(0, GROUPS - 1) as j:
                group(j, False)
            group(GROUPS - 1, True)
            for i in range(2):
                sp.wait_ge(y_out[i], 16 * (4 * GROUPS + 1))

        @block.gpsimd
        def _(pool):
            for n in names:
                pool.sem_inc(S[n], START)
            for o in y_out:
                pool.sem_inc(o, 16)
            pool.memset(pad[:], 0.0).then_inc(S["pad_set"], 1)

            def split_lo(n, slot):
                wait(pool, "hi_done", n + 1)
                nc.gpsimd.tensor_tensor(flat(w_lo[:, slot]), flat(w_raw[:]),
                                        flat(w_hi[:, slot]).bitcast(F32),
                                        ALU.subtract).then_inc(S["lo_done"], 1)

            def per_head(ap):
                return ap.rearrange("p (h c) -> p h c", h=GH)

            def inputs(j, s):
                d, c = where(s)
                if s >= 2:
                    wait(pool, "yd_full", SSM_STEPS * j + (s - 1))
                xv = per_head(x[:, c, :])
                nc.gpsimd.tensor_tensor(per_head(xd[:, s % 2, :]), xv, bcast(gdt[:, c, d, :], HD),
                                        ALU.mult).then_inc(S["xd_ready"], 1)
                if d == 0:
                    nc.gpsimd.tensor_tensor(per_head(y[:, c, :]), xv, bcast(gd[:], HD),
                                            ALU.mult).then_inc(S["y_set"], 1)
                if s % CH < CH - 1:
                    wait(pool, "xd_ready", SSM_STEPS * j + (s + 1))
                    wait(pool, "st_full", NU * j + updates(s))
                    nc.gpsimd.tensor_tensor(per_head(xw[:]), per_head(xd[:, s % 2, :]),
                                            bcast(gin[:, c, d, :], HD),
                                            ALU.mult).then_inc(S["xw_ready"], 1)

            def decayed(j, s):
                if s % CH in (0, CH - 1):
                    return
                d, c = where(s)
                wait(pool, "h_ready", NU * j + updates(s))
                nc.gpsimd.tensor_tensor(per_head(hd[:]), per_head(hs[:, s % 2, :]),
                                        bcast(gtot[:, c, d, :], HD), ALU.mult).then_inc(S["hd_ready"], 1)

            for n in range(XB + 1):
                split_lo(n, n % 2)

            def group(j, last):
                table = SPLIT_LAST if last else SPLIT_AT

                def split(at):
                    if at in table:
                        split_lo(10 * j + (XB + table[at]), table[at] % 2)

                wait(pool, "loc_done", j + 1)
                wait(pool, "xu_free", 8 * j + 8)
                wait(pool, "yf_full", 8 * j)
                inputs(j, 0)
                for s in range(SSM_STEPS):
                    if s + 1 < SSM_STEPS:
                        inputs(j, s + 1)
                    decayed(j, s)
                    split(s)
                split(SSM_STEPS)
                for i in range(8):
                    split(100 + i)
            with pool.Fori(0, GROUPS - 1) as j:
                group(j, False)
            group(GROUPS - 1, True)

        @block.tensor
        def _(pe):
            def project_k(par, slot, half, k):
                for n, (w, h) in enumerate(((w_hi, "h_hi"), (w_hi, "h_lo"), (w_lo, "h_hi"))):
                    last = nc.tensor.matmul(
                        pp[:, par, :], w[:, slot, k, :],
                        keep[h][:, k, half * HALF:(half + 1) * HALF],
                        start=(k == 0 and n == 0), stop=(k == KT - 1 and n == 2))
                if k == KT - 1:
                    last.then_inc(S["pp_full"], 1)

            def project(unit, par, tile, slot, half, part):
                if part == 0:
                    wait(pe, "lo_done", tile + 1)
                    wait(pe, "pp_free", unit - 1)
                for k in (2 * part, 2 * part + 1):
                    project_k(par, slot, half, k)

            def begin(j, s):
                d, c = where(s)
                cols = slice(c * P, c * P + P)
                wait(pe, "exp_done", SSM_STEPS * j + s)
                for h in range(GH):
                    if h % 4 == 0:
                        nc.tensor.matmul(rows[:, h:h + 4, :], ident_r[:],
                                         mask[:, d, :].unsqueeze(1).broadcast_to([P, 4, P]),
                                         start=True, stop=False)
                    one = sel[:, GH * d + h:GH * d + h + 1].broadcast_to([4 * GH, P])
                    last = nc.tensor.matmul(rows[:, h, :], one, crow[:, cols], start=False,
                                            stop=(h % 4 == 3))
                last.then_inc(S["rows_full"], 1)

            def states(j, s):
                if s % CH == CH - 1:
                    return
                n, (_, c) = updates(s), where(s)
                wait(pe, "xw_ready", NU * j + (n + 1))
                wait(pe, "h_ready", NU * j + n)
                nc.tensor.matmul(st_p[:], bc[:, c, 1, :], xw[:], start=True,
                                 stop=True).then_inc(S["st_full"], 1)

            def outputs(j, s):
                d, c = where(s)
                wait(pe, "y_done", SSM_STEPS * j + s)
                if s % CH:
                    wait(pe, "h_ready", NU * j + updates(s))
                    nc.tensor.matmul(yo_p[:], cT[:, c * P:(c + 1) * P], hs[:, s % 2, :], start=True,
                                     stop=True)
                wait(pe, "m_ready", SSM_STEPS * j + (s + 1))
                wait(pe, "xd_ready", SSM_STEPS * j + (s + 1))
                for h in range(GH):
                    last = nc.tensor.matmul(yd_p[:, h * HD:(h + 1) * HD], em[:, s % 2, h, :],
                                            xd[:, s % 2, h * HD:(h + 1) * HD], start=True, stop=True)
                last.then_inc(S["yd_full"], 1)

            def b_and_bc(i, dst):
                b, c = (stage[:, f, i * P:(i + 1) * P] for f in (4, 5))
                nc.tensor.matmul(dst[:, 0, :], b, c, start=True, stop=True)
                nc.tensor.transpose(dst[:, 1, :], b, ident[:]).then_inc(S["xu_full"], 1)

            def unstage(n, i):
                if i == 0:
                    wait(pe, "silu_done", UB * n + UB)
                wait(pe, "xu_free", 8 * n + i)
                for kt in range(4):
                    nc.tensor.transpose(fill[:, 1, kt * P:(kt + 1) * P],
                                        stage[:, kt, i * P:(i + 1) * P], ident[:])
                b_and_bc(i, bc_p[:])

            def first_units(k):
                pe.wait_ge(h_lo, 2 * k + 2)
                if k == 0:
                    wait(pe, "lo_done", 1)
                for half in range(2):
                    project_k(half, 0, half, k)

            for n in range(2 * KT):
                if n >= 2:
                    pe.wait_ge(h_made, n - 1)
                for c in range(4):
                    last = nc.tensor.transpose(fill[:, n % 2, c * P:(c + 1) * P],
                                               x1[:, 4 * (n % 2) + c, n // 2 * P:n // 2 * P + P],
                                               ident[:])
                last.then_inc(t_full, 1)
                if n % 2 and n > 1:
                    first_units(n // 2 - 1)
            first_units(KT - 1)
            pe.wait_ge(const_in, CONSTS)
            for c in range(CH):
                for k in range(KT):
                    for n, h in enumerate(("h_hi", "h_lo")):
                        last = nc.tensor.matmul(
                            dp[:, c, :], keep[h][:, k, c * P:(c + 1) * P].bitcast(F32), wd[:, k, :],
                            start=(k == 0 and n == 0), stop=(k == KT - 1 and n == 1))
            last.then_inc(dt_full, 1)
            for u in range(2, UB):
                for part in range(4):
                    project(u, u % 2, u // 2, u // 2 % 2, u % 2, part)
                if u == 3:
                    pe.wait_ge(ac_ready, 1)
                    cum = cum_p[:].rearrange("p (c d h) -> p d c h", c=CH, d=2)
                    nc.tensor.matmul(cum[:, 0], tri[:, 0, :], ac[:, :, 0:SH], start=True, stop=True)
                    nc.tensor.matmul(cum[:, 1], tri[:, 1, :], ac[:, :, SH:W2], start=True, stop=True)
                    nc.tensor.matmul(tot_p[:], tri[:, 2, :], xw[:], start=True,
                                     stop=True).then_inc(cum_full, 1)
                if u == 5:
                    pe.wait_ge(cum_ready, 1)
                    for c in range(CH):
                        last = nc.tensor.transpose(fill[0:W2, c // 4, c % 4 * P:(c % 4 + 1) * P],
                                                   keep["cum"][:, c, :], ident[:])
                    last.then_inc(row_full, 1)
            pe.wait_ge(row_lo_done, 2)
            wait(pe, "silu_done", 8)
            for i in range(8):
                if i >= 2:
                    pe.wait_ge(first_x_moved, i - 1)
                for kt in range(4):
                    last = nc.tensor.transpose(fill[:, i % 2, kt * P:(kt + 1) * P],
                                               stage[:, kt, i * P:(i + 1) * P], ident[:])
                last.then_inc(first_x_full, 1)
            wait(pe, "silu_done", UB)
            for i in range(8):
                if i >= 2:
                    wait(pe, "xu_free", i - 1)
                b_and_bc(i, (bc_p[:], bc_p2)[i % 2])
            wait(pe, "sel_done", 1)

            def group(j, last):
                units = 20 * j + UB

                def quarter(q):
                    if last:
                        if q % QPS == 1:
                            return
                        q = 2 * (q // QPS) + q % QPS // 2
                        u = q // 4
                        project(units + u, u % 2, 10 * j + (XB + u // 2), u // 2 % 2, u % 2, q % 4)
                    else:
                        u = q // 4
                        project(units + u, u % 2, 10 * j + (XB + u // 2), u // 2 % 2, u % 2, q % 4)

                wait(pe, "xu_free", 8 * j + 8)
                wait(pe, "y_gated", 8 * j)
                wait(pe, "c_moved", j + 1)
                pe.wait_ge(crow_in, 64 * j + 64)
                begin(j, 0)
                for s in range(SSM_STEPS):
                    quarter(QPS * s)
                    if s + 1 < SSM_STEPS:
                        begin(j, s + 1)
                    states(j, s)
                    quarter(QPS * s + 1)
                    outputs(j, s)
                    quarter(QPS * s + 2)
                zu = units + UB
                wait(pe, "exp_done", SSM_STEPS * j + SSM_STEPS)
                for i in range(8):
                    f = i // 2 + XB
                    tile, slot = 10 * j + (XB + f), f % 2
                    if not last:
                        project(zu + i, i % 2, tile, slot, i % 2, 0)
                        project(zu + i, i % 2, tile, slot, i % 2, 1)
                    if i == 0:
                        wait(pe, "y_done", SSM_STEPS * j + SSM_STEPS)
                    wait(pe, "y_gated", 8 * j + i)
                    for c in range(4):
                        last_t = nc.tensor.transpose(
                            fill[:, 0, c * P:(c + 1) * P],
                            y[:, 4 * (i % 2) + c, i // 2 * P:(i // 2 + 1) * P], ident[:])
                    last_t.then_inc(S["yf_full"], 1)
                    if not last and i >= 1:
                        unstage(j + 1, i - 1)
                    if not last:
                        project(zu + i, i % 2, tile, slot, i % 2, 2)
                        project(zu + i, i % 2, tile, slot, i % 2, 3)
                if not last:
                    unstage(j + 1, 7)
            with pe.Fori(0, GROUPS - 1) as j:
                group(j, False)
            group(GROUPS - 1, True)

        @block.scalar
        def _(act):
            def put(dst, src, **kw):
                return nc.scalar.activation(dst, src, ACT.Copy, **kw)

            def split_hi(n, slot):
                act.wait_ge(w_in, 16 * n + 16)
                wait(act, "pp_full", 2 * n - 2)
                put(flat(w_hi[:, slot]), flat(w_raw[:])).then_inc(S["hi_done"], 1)

            def to_pad(unit, tile, par, half):
                wait(act, "pp_full", unit + 1)
                if half == 0:
                    wait(act, "conv_done", tile)
                t0 = TAPS // 2 + half * HALF
                put(pad[:, t0:t0 + HALF], pp[:, par, :]).then_inc(S["pp_free"], 1)

            def tanh(tile, f):
                wait(act, "conv_done", tile + 1)
                wait(act, "silu_done", 2 * tile)
                for h in range(2):
                    nc.scalar.activation(th[:, h, :], stage[:, f, h * HALF:(h + 1) * HALF],
                                         ACT.Tanh).then_inc(S["tanh_done"], 1)

            def conv_weights(g):
                src = conv[:, g, :] if isinstance(g, int) else conv[:, bass.ds(g, 1), :].rearrange(
                    "p a c -> p (a c)")
                wait(act, "conv_done", XB * g)
                put(gconv[:], src, scale=0.5).then_inc(S["gconv_done"], 1)

            def factors(j):
                wait(act, "y_done", SSM_STEPS * j)
                cum, dif, tot, dt = (keep[n][:].rearrange("p c (d h) -> p c d h", d=2)
                                     [:, :, :, bass.ds(j * GH, GH)]
                                     for n in ("cum", "dif", "tot", "dt"))
                for d in range(2):
                    put(gneg[:, :, d, :], cum[:, :, d, :], scale=-1.0)
                    put(gdt[:, :, d, :], dt[:, :, d, :])
                    nc.scalar.activation(gout[:, :, d, :], cum[:, :, d, :], ACT.Exp)
                    nc.scalar.activation(gin[:, :, d, :], dif[:, :, d, :], ACT.Exp)
                    nc.scalar.activation(gtot[:, :, d, :], tot[:, :, d, :], ACT.Exp)
                put(gd[:], dskip[:, bass.ds(j * GH, GH)]).then_inc(S["loc_done"], 1)

            def move_c(n):
                wait(act, "silu_done", UB * n + UB)
                wait(act, "y_done", SSM_STEPS * n)
                put(cT[:], stage[:, 5, :]).then_inc(S["c_moved"], 1)

            def unstaged(n, i):
                wait(act, "xu_full", 8 * n + (i + 1))
                if i == 0:
                    wait(act, "y_done", SSM_STEPS * n)
                    wait(act, "xd_ready", SSM_STEPS * n)
                put(x[:, i, :], fill[:, 1, :])
                put(bc[:, i], bc_p[:]).then_inc(S["xu_free"], 1)

            def exponentials(j, s):
                d, c = where(s)
                wait(act, "rows_full", SSM_STEPS * j + (s + 1))
                wait(act, "yd_full", SSM_STEPS * j + (s - 1))
                for h in range(GH):
                    last = nc.scalar.activation(em[:, s % 2, h, :], rows[:, h, :], ACT.Exp,
                                                bias=gneg[:, c, d, h:h + 1])
                last.then_inc(S["exp_done"], 1)

            for n in range(2 * KT):
                k, t0 = n // 2, n % 2 * HALF
                act.wait_ge(t_full, n + 1)
                if n >= 2:
                    act.wait_ge(h_lo, n - 1)
                nc.scalar.activation(h_tmp[:, n % 2, :], fill[:, n % 2, :], ACT.Identity,
                                     bias=keep["mods"][:, 1, k:k + 1],
                                     scale=keep["mods"][:, 1, KT + k:KT + k + 1]).then_inc(h_made, 1)
                act.wait_ge(h_made, n + 1)
                put(keep["h_hi"][:, k, t0:t0 + HALF], h_tmp[:, n % 2, :]).then_inc(h_hi, 1)
                if n == 1:
                    split_hi(0, 0)
            split_hi(1, 1)
            act.wait_ge(const_in, CONSTS)
            conv_weights(0)
            put(ident_r[:], ident[:])
            put(mask[:], mask_raw)
            put(sel[:], sel_raw[:]).then_inc(S["sel_done"], 1)
            wait(act, "pad_set", 1)
            for f in range(XB):
                n = f + 1
                if 1 < n < XB:
                    split_hi(n, n % 2)
                for h in range(2):
                    to_pad(2 * f + h, f, h, h)
                tanh(f, f)
                if f == 0:
                    nc.scalar.activation(arow, arow, ACT.Exp).then_inc(a_done, 1)
                    act.wait_ge(neg_abs, 1)
                    nc.scalar.activation(e, e, ACT.Exp).then_inc(exped, 1)
                    act.wait_ge(logged, 1)
                    nc.scalar.activation(lg, r, ACT.Ln).then_inc(exped, 1)
                if f == 2:
                    act.wait_ge(row_full, 1)
                    for n in range(2):
                        put(row_hi[:, n * HALF:(n + 1) * HALF].bitcast(F32R),
                            fill[0:W2, n, :]).then_inc(row_hi_done, 1)
            split_hi(XB, 0)
            for i in range(8):
                act.wait_ge(first_x_full, i + 1)
                put(x[:, i, :], fill[:, i % 2, :]).then_inc(first_x_moved, 1)
            for i in range(8):
                wait(act, "xu_full", i + 1)
                put(bc[:, i], (bc_p[:], bc_p2)[i % 2]).then_inc(S["xu_free"], 1)
            act.wait_ge(row_out, 32)
            move_c(0)
            act.wait_ge(sums_done, 1)
            factors(0)

            def group(j, last):
                units = 20 * j + UB
                table = SPLIT_LAST if last else SPLIT_AT

                def split(at):
                    if at in table:
                        split_hi(10 * j + (XB + table[at]), table[at] % 2)

                wait(act, "loc_done", j + 1)
                if not last:
                    conv_weights(j + 1)
                exponentials(j, 0)
                for s in range(SSM_STEPS + 1):
                    if s + 1 < SSM_STEPS:
                        exponentials(j, s + 1)
                    if not last:
                        for u in EVAC_STEP.get(s, ()):
                            to_pad(units + u, XB * j + (XB + u // 2), u % 2, u % 2)
                    split(s)
                    if last and s in Z_STEP:
                        u = Z_STEP[s]
                        wait(act, "pp_full", units + (u + 1))
                        if u >= 2:
                            wait(act, "z_done", u - 1)
                        nc.scalar.activation(th[:, u % 2, :], pp[:, u % 2, :], ACT.Tanh, scale=0.5)
                        put(zs[:, u % 2, :], pp[:, u % 2, :], scale=0.5).then_inc(S["pp_free"], 1)
                    if not last and s - 1 in CONV_STEP:
                        f = CONV_STEP[s - 1]
                        tanh(XB * j + (XB + f), f)
                if last:
                    return
                zu = units + UB
                wait(act, "yd_full", SSM_STEPS * j + SSM_STEPS)
                for i in range(8):
                    split(100 + i)
                    if i >= 1:
                        unstaged(j + 1, i - 1)
                    wait(act, "pp_full", zu + (i + 1))
                    wait(act, "y_gated", 8 * j + (i - 1 if i >= 2 else 0))
                    nc.scalar.activation(th_z[:, i % 2, :], pp[:, i % 2, :], ACT.Tanh, scale=0.5)
                    put(zs[:, i % 2, :], pp[:, i % 2, :], scale=0.5).then_inc(S["pp_free"], 1)
                    if i == 0:
                        tanh(XB * j + (XB + 5), 5)
                        factors(j + 1)
                unstaged(j + 1, 7)
                move_c(j + 1)
            with act.Fori(0, GROUPS - 1) as j:
                group(j, False)
            group(GROUPS - 1, True)

        @block.vector
        def _(dve):
            def per_head(ap):
                return ap.rearrange("p (h c) -> p h c", h=GH)

            def weigh(ch, j, s):
                _, c = where(s)
                wait(dve, "exp_done", SSM_STEPS * j + (s + 1))
                nc.vector.tensor_tensor(em[:, s % 2], em[:, s % 2],
                                        bc[:, c, 0, :].unsqueeze(1).broadcast_to([P, GH, P]),
                                        ALU.mult).then_inc(S["m_ready"], 1)

            def update(ch, j, s):
                if s % CH == CH - 1:
                    return
                n = updates(s)
                wait(dve, "st_full", NU * j + (n + 1))
                if s % CH == 0:
                    nc.vector.tensor_copy(hs[:, (s + 1) % 2, :], st_p[:]).then_inc(S["h_ready"], 1)
                else:
                    wait(dve, "hd_ready", 12 * j + (6 * (s // CH) + s % CH))
                    nc.vector.tensor_tensor(hs[:, (s + 1) % 2, :], hd[:], st_p[:],
                                            ALU.add).then_inc(S["h_ready"], 1)

            def assemble(ch, j, s):
                d, c = where(s)
                wait(dve, "yd_full", SSM_STEPS * j + (s + 1))
                wait(dve, "y_set", 8 * j + (s + 1 if d == 0 else 8))
                if s % CH == 0:
                    nc.vector.tensor_tensor(y[:, c, :], y[:, c, :], yd_p[:],
                                            ALU.add).then_inc(S["y_done"], 1)
                else:
                    ch.link(nc.vector.tensor_tensor(per_head(yt[:]), per_head(yo_p[:]),
                                                    bcast(gout[:, c, d, :], HD), ALU.mult))
                    ch.link(nc.vector.tensor_tensor(yt[:], yt[:], yd_p[:], ALU.add))
                    nc.vector.tensor_tensor(y[:, c, :], y[:, c, :], yt[:],
                                            ALU.add).then_inc(S["y_done"], 1)
                wait(dve, "y_done", SSM_STEPS * j + (s + 1))

            def convolve(ch, tile, unit, f, k0=0, k1=TAPS):
                w = gconv[:, (TAPS + 1) * f:(TAPS + 1) * (f + 1)]
                out = stage[:, f, :]
                for k in range(k0, k1):
                    if k == 0:
                        wait(dve, "pp_free", unit + 1)
                        ins = nc.vector.tensor_scalar(out, pad[:, 0:SEQ], w[:, 0:1],
                                                      w[:, TAPS:TAPS + 1], ALU.mult, ALU.add)
                    else:
                        ins = nc.vector.scalar_tensor_tensor(out, pad[:, k:k + SEQ], w[:, k:k + 1],
                                                             out, ALU.mult, ALU.add)
                    if k < TAPS - 1:
                        ch.link(ins)
                    else:
                        ins.then_inc(S["conv_done"], 1)

            def silu(tile, f):
                for h in range(2):
                    wait(dve, "tanh_done", 2 * tile + (h + 1))
                    v = stage[:, f, h * HALF:(h + 1) * HALF]
                    nc.vector.scalar_tensor_tensor(v, th[:, h, :], 1.0, v, ALU.add,
                                                   ALU.mult).then_inc(S["silu_done"], 1)

            for n in range(2 * KT):
                k, t0 = n // 2, n % 2 * HALF
                dve.wait_ge(h_hi, n + 1)
                nc.vector.tensor_tensor(keep["h_lo"][:, k, t0:t0 + HALF], h_tmp[:, n % 2, :],
                                        keep["h_hi"][:, k, t0:t0 + HALF].bitcast(F32),
                                        ALU.subtract).then_inc(h_lo, 1)

            def decays():
                dc = Chain(dve, d_step, 0)
                dve.wait_ge(dt_full, 1)
                W = [P, CH, W2]
                dc.link(nc.vector.tensor_tensor(v, dp, brow.unsqueeze(1).broadcast_to(W), ALU.add))
                dc.link(nc.vector.tensor_scalar(r, v, -1.0, None, ALU.mult))
                nc.vector.tensor_tensor(e, v, r, ALU.min).then_inc(neg_abs, 1)
                dve.wait_ge(exped, 1)
                nc.vector.tensor_scalar(r, e, 1.0, None, ALU.add).then_inc(logged, 1)
                dve.wait_ge(logged, 1)
                dve.wait_ge(exped, 2)
                dc.link(nc.vector.tensor_scalar(r, r, -1.0, None, ALU.add))
                dc.link(nc.vector.tensor_scalar(m, r, 0.0, None, ALU.is_equal))
                dc.link(nc.vector.tensor_tensor(r, r, m, ALU.add))
                dc.link(nc.vector.reciprocal(r, r))
                dc.link(nc.vector.tensor_tensor(m, m, lg, ALU.add))
                dc.link(nc.vector.tensor_tensor(m, m, e, ALU.mult))
                dc.link(nc.vector.tensor_tensor(m, m, r, ALU.mult))
                dc.link(nc.vector.tensor_scalar(v, v, 0.0, None, ALU.max))
                dc.link(nc.vector.tensor_tensor(keep["dt"][:], v, m, ALU.add))
                dve.wait_ge(a_done, 1)
                nc.vector.scalar_tensor_tensor(ac, keep["dt"][:], -1.0,
                                               arow.unsqueeze(1).broadcast_to(W), ALU.mult,
                                               ALU.mult).then_inc(ac_ready, 1)
                dve.wait_ge(cum_full, 1)
                nc.vector.tensor_copy(keep["tot"][:], by_chunk(tot_p[:]))
                nc.vector.tensor_copy(keep["cum"][:], by_chunk(cum_p[:])).then_inc(cum_ready, 1)
                dve.wait_ge(cum_ready, 1)
                nc.vector.tensor_tensor(keep["dif"][:], keep["tot"][:], keep["cum"][:],
                                        ALU.subtract).then_inc(sums_done, 1)

            dve.wait_ge(const_in, CONSTS)
            wait(dve, "pad_set", 1)
            wait(dve, "gconv_done", 1)
            ch0 = Chain(dve, S["v_step"], START)
            for f in range(XB):
                convolve(ch0, f, 2 * f + 1, f)
                silu(f, f)
                if f == 0:
                    decays()
                if f == 2:
                    for n in range(2):
                        half = slice(n * HALF, (n + 1) * HALF)
                        dve.wait_ge(row_hi_done, n + 1)
                        nc.vector.tensor_tensor(row_lo[:, half].bitcast(F32R), fill[0:W2, n, :],
                                                row_hi[:, half], ALU.subtract
                                                ).then_inc(row_lo_done, 1)
            def silu_z(units, u):
                wait(dve, "pp_free", units + (u + 1))
                nc.vector.scalar_tensor_tensor(z_of(u), th[:, u % 2, :], 1.0, zs[:, u % 2, :],
                                               ALU.add, ALU.mult).then_inc(S["z_done"], 1)

            steps0 = ch0.n
            STEPS = 28 + 4 * XB + 8

            def group(j, last):
                ch = Chain(dve, S["v_step"], START + steps0 + STEPS * j)
                units = 20 * j + UB
                wait(dve, "loc_done", j + 1)
                wait(dve, "xu_free", 8 * j + 8)
                weigh(ch, j, 0)
                wait(dve, "xu_full", 8 * j + 8)
                if not last:
                    wait(dve, "gconv_done", j + 2)
                    wait(dve, "c_moved", j + 1)
                for s in range(SSM_STEPS):
                    update(ch, j, s)
                    if not last and s - 1 in CONV_STEP:
                        f = CONV_STEP[s - 1]
                        convolve(ch, XB * j + (XB + f), units + 2 * f + 1, f, 2, TAPS)
                    if s + 1 < SSM_STEPS:
                        weigh(ch, j, s + 1)
                    assemble(ch, j, s)
                    if last and s in Z_STEP:
                        silu_z(units, Z_STEP[s])
                    if not last:
                        if s in CONV_STEP:
                            f = CONV_STEP[s]
                            convolve(ch, XB * j + (XB + f), units + 2 * f + 1, f, 0, 2)
                        if s - 1 in CONV_STEP:
                            f = CONV_STEP[s - 1]
                            silu(XB * j + (XB + f), f)
                if not last:
                    convolve(ch, XB * j + (XB + 5), units + 11, 5)
                if last:
                    silu_z(units, 7)
                    wait(dve, "z_done", 8)
                zu = units + UB
                for i in range(8):
                    if not last:
                        wait(dve, "pp_free", zu + (i + 1))
                        ch.link(nc.vector.scalar_tensor_tensor(
                            zs[:, i % 2, :], th_z[:, i % 2, :], 1.0, zs[:, i % 2, :], ALU.add, ALU.mult))
                    z = z_of(i) if last else zs[:, i % 2, :]
                    wait(dve, "yf_full", 8 * j + (i + 1))
                    dve.wait_ge(y_out[i % 2], 64 * j + 16 * (i // 2 + 1))
                    nc.vector.tensor_tensor(yst[:, i % 2, :], fill[:, 0, :], z,
                                            ALU.mult).then_inc(S["y_gated"], 1)
                    if i == 0 and not last:
                        silu(XB * j + (XB + 5), 5)
                if not last:
                    assert ch.n == STEPS, ch.n
            with dve.Fori(0, GROUPS - 1) as j:
                group(j, False)
            group(GROUPS - 1, True)

def build(nc, io, out):
    def scratch(name, shape):
        return nc.dram_tensor(name, shape, F32, kind="Internal").ap()

    io["gate_row"] = scratch("gate_row", (DEPTH, D))
    io["x1"] = scratch("x1", (SEQ // P, P, D))
    io["cum_rows"] = scratch("cum_rows", (2, 2 * SH, SEQ))
    io["yT"] = scratch("yT_b", (SEQ // P, P, 2 * KT, P))
    with ExitStack() as ctx:
        def held(name, shape, dt=F32, scope=ctx):
            return scope.enter_context(nc.sbuf_tensor(name, shape, dt))

        keep = {"mods": held("mods", [P, DEPTH, 2 * KT]), "cond": held("cond", [P, KT]),
                "ident": held("ident", [P, P]),
                "trunk": held("trunk", [P, SEQ * KT])}

        def split_h(scope, layer):
            for n in ("h_hi", "h_lo"):
                keep[n] = held(f"{n}{layer}", [P, KT, SEQ], F32R, scope)

        with ExitStack() as scope:
            split_h(scope, 0)
            keep["w_raw"] = held("w_raw", [P, 2, KT, P], F32, scope)
            keep["w_hi"] = held("w_hi", [P, 2, KT, P], F32R, scope)
            keep["w_lo"] = held("w_lo", [P, 2, KT, P], F32R, scope)
            modulation_phase(nc, io, keep)
            with nc.cleanup_on_exit():
                attention_phase(nc, io, keep)
        io["x_rows"], io["x_out"], io["w_out"] = io["x"], io["x1"], io["a_w_out"]
        output_phase(nc, io, keep, 0)
        io["x_rows"] = io["x1"]
        with ExitStack() as scope:
            split_h(scope, 1)
            for n in ("cum", "dif", "tot", "dt"):
                keep[n] = held(f"all_{n}", [P, CH, 2 * SH], F32, scope)
            state_space_phase(nc, io, keep)
        io["x_out"], io["w_out"] = out, io["b_w_out"]
        output_phase(nc, io, keep, 1)

def kernel(**inputs):
    import numpy as _np
    import concourse.bacc as _bacc
    from concourse.bass_utils import run_bass_kernel_spmd as _run

    nc = _bacc.Bacc("TRN2", target_bir_lowering=False, num_devices=1)
    arrays, io = {}, {}

    def given(name, a):
        a = _np.ascontiguousarray(a)
        arrays[f"in_{name}"] = a
        io[name] = nc.dram_tensor(f"in_{name}", a.shape, F32, kind="ExternalInput").ap()

    def tiles(w, cols, width=P):
        k = w.shape[0] // P
        w = w.reshape(k, P, w.shape[1])
        return _np.stack([w[:, :, c:c + width].transpose(1, 0, 2) for c in cols])

    g = {n: _np.asarray(v) for n, v in inputs.items()}
    x = g["x"][0]
    given("x", x.reshape(SEQ // P, P, D))
    given("xT", x.T.reshape(KT, P, SEQ).transpose(1, 0, 2))
    given("c", g["c"].reshape(KT, P).T)
    given("ada_w", g["ada_w"])
    given("ada_b", g["ada_b"][None])
    given("ada_b_cols", g["ada_b"][:, :2 * D].reshape(DEPTH, 2 * KT, P).transpose(0, 2, 1))
    given("ln_g", g["ln_g"])
    given("ln_b", g["ln_b"])
    given("a_w", tiles(g["a_w_in"][0], stream_a()))
    given("a_w_out", g["a_w_out"][0])

    given("b_w", tiles(g["b_w_in"][0], stream_b()).reshape(10 * GROUPS, P, KT * P))
    given("w_dt", tiles(g["b_w_in"][0], [2 * SSM_INNER + 2 * GROUPS * NS],
                        2 * SH)[0])
    given("b_w_out", g["b_w_out"][0])
    given("dt_bias", g["b_dt_bias"].reshape(1, 2 * SH))
    given("a_log", g["b_a_log"].reshape(1, 2 * SH))
    given("d_skip", g["b_d"])
    given("norm_w", g["b_norm_w"][0].reshape(2 * KT, P).T)
    cw = _np.concatenate([g["b_conv_w"][0], g["b_conv_b"]], 0)
    cw = _np.stack([cw[:, c:c + P] for c in conv_channels()])
    given("conv", cw.transpose(2, 0, 1).reshape(P, GROUPS, XB * (TAPS + 1)))
    s, t = _np.arange(P)[:, None], _np.arange(P)[None, :]
    given("tri", _np.stack([s <= t, s >= t, s == s + 0 * t], 1).astype(_np.float32))
    given("mask", _np.stack([_np.where(t >= s, 0.0, MASKED), _np.where(t <= s, 0.0, MASKED)],
                            1).astype(_np.float32))
    given("sel", _np.tile(_np.eye(2 * GH, dtype=_np.float32), (2, 1)))

    slope = 2.0 ** (-8.0 * (_np.arange(2, dtype=_np.float32) + 1.0) / HEADS)
    rows = _np.repeat(slope, HD)[:, None]
    given("bias", bias_tables())
    given("ident", _np.eye(P, dtype=_np.float32))
    given("slope", _np.tile(slope[None, :], (P, 1)).astype(_np.float32))
    given("qscale", _np.concatenate([1 / (8 * rows), 2 / (8 * rows)], 1).astype(_np.float32))

    out = nc.dram_tensor("out", (SEQ // P, P, D), F32, kind="ExternalOutput").ap()
    build(nc, io, out)
    r = _run(nc, [arrays], core_ids=[0])
    return _np.asarray(r.results[0]["out"]).reshape(1, SEQ, D)
```
